# Optimizing a Trainium2 kernel written in Bass

```python
import jax, jax.numpy as jnp
from jax import lax
import numpy as np

D_MODEL = 1024
BATCH = 1
SEQ = 1024
DEPTH = 1

CHUNK = 64
N_MEM = 256
HGRN_HEADS = 4
HGRN_DK = 128
HGRN_DV = 128
HGRN_QK = HGRN_HEADS * HGRN_DK
HGRN_WIDTH = HGRN_HEADS * HGRN_DV
SB_HEADS = 8
SB_HEAD_DIM = 64
SB_WIDTH = SB_HEADS * SB_HEAD_DIM
SB_BLOCK = 128
XATTN_HEADS = 4
XATTN_HEAD_DIM = D_MODEL // XATTN_HEADS
D_FF = ((8 * D_MODEL // 3 + 255) // 256) * 256
EPS = 1e-6
IN_SIZES = (HGRN_QK, HGRN_QK, HGRN_WIDTH, HGRN_WIDTH, SB_WIDTH, SB_WIDTH, SB_WIDTH)
IN_OFFSETS = tuple(int(v) for v in np.cumsum(IN_SIZES)[:-1])
D_IN = int(sum(IN_SIZES))

kernel_name = 'hybrid_hgrn2_stickbreaking_xattn_block'

def rms_norm(x, gain):
    xf = x.astype(jnp.float32)
    y = xf * lax.rsqrt(jnp.mean(xf * xf, axis=-1, keepdims=True) + EPS)
    return (y * gain.astype(jnp.float32)).astype(x.dtype)

def hgrn2_mixer(q, f_pre, i, g, lb, norm_gain):
    B, T, _ = q.shape
    nc = T // CHUNK
    f32 = jnp.float32
    lbf = lb.astype(f32)
    q = jax.nn.silu(q.astype(f32))
    f = lbf + (1.0 - lbf) * jax.nn.sigmoid(f_pre.astype(f32))
    k = 1.0 - f
    log_f = jnp.log(f)

    def to_chunks(t, d):
        return t.reshape(B, nc, CHUNK, HGRN_HEADS, d).transpose(1, 0, 3, 2, 4)

    qc = to_chunks(q, HGRN_DK)
    kc = to_chunks(k, HGRN_DK)
    lfc = to_chunks(log_f, HGRN_DK)
    vc = to_chunks(i.astype(f32), HGRN_DV)
    tri = jnp.tril(jnp.ones((CHUNK, CHUNK), dtype=bool))[:, :, None]

    def step(S, xs):
        q_c, k_c, lf_c, v_c = xs
        b = jnp.cumsum(lf_c, axis=-2)
        diff = b[:, :, :, None, :] - b[:, :, None, :, :]
        decay = jnp.where(tri, jnp.exp(jnp.where(tri, diff, 0.0)), 0.0)
        scores = jnp.einsum('bhtd,bhsd,bhtsd->bhts', q_c, k_c, decay)
        o = (jnp.einsum('bhts,bhsv->bhtv', scores, v_c)
             + jnp.einsum('bhtd,bhdv->bhtv', q_c * jnp.exp(b), S))
        b_last = b[:, :, -1:, :]
        S = (jnp.exp(b_last[:, :, 0, :])[..., None] * S
             + jnp.einsum('bhsd,bhsv->bhdv', k_c * jnp.exp(b_last - b), v_c))
        return S, o

    S0 = jnp.zeros((B, HGRN_HEADS, HGRN_DK, HGRN_DV), f32)
    _, o = lax.scan(step, S0, (qc, kc, lfc, vc))
    o = o.transpose(1, 0, 3, 2, 4).reshape(B, T, HGRN_HEADS, HGRN_DV)
    o = rms_norm(o, norm_gain.reshape(HGRN_HEADS, HGRN_DV)).reshape(B, T, HGRN_WIDTH)
    return (o * jax.nn.silu(g.astype(f32))).astype(g.dtype)

def stick_breaking_mixer(q, k, v):
    B, T, _ = q.shape
    f32 = jnp.float32
    nq = T // SB_BLOCK
    scale = SB_HEAD_DIM ** -0.5
    qh = q.astype(f32).reshape(B, T, SB_HEADS, SB_HEAD_DIM).transpose(0, 2, 1, 3)
    kh = k.astype(f32).reshape(B, T, SB_HEADS, SB_HEAD_DIM).transpose(0, 2, 1, 3)
    vh = v.astype(f32).reshape(B, T, SB_HEADS, SB_HEAD_DIM).transpose(0, 2, 1, 3)
    qb = qh.reshape(B, SB_HEADS, nq, SB_BLOCK, SB_HEAD_DIM).transpose(2, 0, 1, 3, 4)
    key_pos = jnp.arange(T)

    def block(args):
        q_blk, blk = args
        z = jnp.einsum('bhqd,bhkd->bhqk', q_blk, kh) * scale
        q_pos = blk * SB_BLOCK + jnp.arange(SB_BLOCK)
        causal = key_pos[None, :] < q_pos[:, None]
        log_rest = jnp.where(causal, jax.nn.log_sigmoid(-z), 0.0)
        between = lax.cumsum(log_rest, axis=3, reverse=True) - log_rest
        log_a = jax.nn.log_sigmoid(z) + between
        a = jnp.where(causal, jnp.exp(log_a), 0.0)
        return jnp.einsum('bhqk,bhkd->bhqd', a, vh)

    o = lax.map(block, (qb, jnp.arange(nq)))
    o = o.transpose(1, 0, 3, 2, 4).reshape(B, T, SB_WIDTH)
    return o.astype(q.dtype)

def cross_attention(h, m, w_q, w_kv, w_o):
    B, T, _ = h.shape
    f32 = jnp.float32
    q = (h @ w_q).reshape(B, T, XATTN_HEADS, XATTN_HEAD_DIM)
    k, v = jnp.split(m @ w_kv, 2, axis=-1)
    k = k.reshape(B, N_MEM, XATTN_HEADS, XATTN_HEAD_DIM)
    v = v.reshape(B, N_MEM, XATTN_HEADS, XATTN_HEAD_DIM)
    s = jnp.einsum('bthd,bnhd->bhtn', q.astype(f32), k.astype(f32)) * (XATTN_HEAD_DIM ** -0.5)
    p = jax.nn.softmax(s, axis=-1)
    o = jnp.einsum('bhtn,bnhd->bthd', p, v.astype(f32)).reshape(B, T, D_MODEL)
    return o.astype(h.dtype) @ w_o

def swiglu(h, w_in, w_out):
    gate, up = jnp.split(h @ w_in, 2, axis=-1)
    return (jax.nn.silu(gate) * up) @ w_out

def setup_inputs(seed: int = 0) -> dict:
    key = jax.random.key(seed)
    ks = jax.random.split(key, 20)

    def w(k, shape, fan_in):
        return jax.random.normal(k, shape, jnp.float32) * fan_in ** -0.5

    def gain(k, shape):
        return 1.0 + 0.02 * jax.random.normal(k, shape, jnp.float32)

    return dict(
        x=jax.random.normal(ks[0], (BATCH, SEQ, D_MODEL), jnp.float32),
        mem=jax.random.normal(ks[1], (BATCH, N_MEM, D_MODEL), jnp.float32),
        g_mix=gain(ks[2], (DEPTH, D_MODEL)),
        w_in=w(ks[3], (DEPTH, D_MODEL, D_IN), D_MODEL),
        lb_table=0.5 * jax.random.normal(ks[4], (DEPTH + 1, HGRN_QK), jnp.float32),
        g_hgrn=gain(ks[5], (DEPTH, HGRN_WIDTH)),
        w_gate=w(ks[6], (DEPTH, D_MODEL, 2 * D_MODEL), D_MODEL),
        w_proj_a=w(ks[7], (DEPTH, HGRN_WIDTH, D_MODEL), HGRN_WIDTH),
        w_proj_b=w(ks[8], (DEPTH, SB_WIDTH, D_MODEL), SB_WIDTH),
        w_out=w(ks[9], (DEPTH, D_MODEL, D_MODEL), D_MODEL),
        g_xattn=gain(ks[10], (DEPTH, D_MODEL)),
        g_mem=gain(ks[11], (DEPTH, D_MODEL)),
        w_xq=w(ks[12], (DEPTH, D_MODEL, D_MODEL), D_MODEL),
        w_xkv=w(ks[13], (DEPTH, D_MODEL, 2 * D_MODEL), D_MODEL),
        w_xo=w(ks[14], (DEPTH, D_MODEL, D_MODEL), D_MODEL),
        g_ffn=gain(ks[15], (DEPTH, D_MODEL)),
        w_ffn_in=w(ks[16], (DEPTH, D_MODEL, 2 * D_FF), D_MODEL),
        w_ffn_out=w(ks[17], (DEPTH, D_FF, D_MODEL), D_FF),
        g_final=gain(ks[18], (D_MODEL,)),
    )

def reference(x, mem, g_mix, w_in, lb_table, g_hgrn, w_gate, w_proj_a, w_proj_b, w_out,
              g_xattn, g_mem, w_xq, w_xkv, w_xo, g_ffn, w_ffn_in, w_ffn_out, g_final):
    lb_all = jnp.cumsum(jax.nn.softmax(lb_table.astype(jnp.float32), axis=0), axis=0)
    for l in range(DEPTH):
        h = rms_norm(x, g_mix[l])
        q_a, f_a, i_a, o_a, q_b, k_b, v_b = jnp.split(h @ w_in[l], IN_OFFSETS, axis=-1)
        y_a = hgrn2_mixer(q_a, f_a, i_a, o_a, lb_all[l], g_hgrn[l])
        y_b = stick_breaking_mixer(q_b, k_b, v_b)
        gate_a, gate_b = jnp.split(jax.nn.sigmoid(h @ w_gate[l]), 2, axis=-1)
        merged = gate_a * (y_a @ w_proj_a[l]) + gate_b * (y_b @ w_proj_b[l])
        x = x + merged @ w_out[l]
        x = x + cross_attention(rms_norm(x, g_xattn[l]), rms_norm(mem, g_mem[l]),
                                w_xq[l], w_xkv[l], w_xo[l])
        x = x + swiglu(rms_norm(x, g_ffn[l]), w_ffn_in[l], w_ffn_out[l])
    return rms_norm(x, g_final)


_drawn_inputs = setup_inputs


def setup_inputs(seed=0):
    import zlib

    import numpy as np

    out = dict(_drawn_inputs(seed))
    spreads = {}
    factors = {'g_mix': 4.231,
     'lb_table': 2.915,
     'g_hgrn': 8.0,
     'g_xattn': 8.0,
     'g_mem': 8.0,
     'g_ffn': 14.431,
     'g_final': 8.453}
    for name, (base, spread) in spreads.items():
        noise = np.random.default_rng([zlib.crc32(name.encode()), seed]).standard_normal(out[name].shape)
        drawn = base * np.exp(spread * noise) if base else spread * noise
        out[name] = __import__('jax').numpy.asarray(drawn.astype(out[name].dtype))
    for name, factor in factors.items():
        out[name] = (out[name] * factor).astype(out[name].dtype)
    return out
```

```python
from contextlib import ExitStack

import concourse.bass as bass
from concourse import mybir
import numpy as np

ALU = mybir.AluOpType
ACT = mybir.ActivationFunctionType
F32 = mybir.dt.float32
F32R = mybir.dt.float32r
I32 = mybir.dt.int32
AX_X = mybir.AxisListType.X

P = 128
D = 1024
T = 1024
KT = D // P
HALF = 512
M = 256
HEADS = 4
CH = 128
NCH = T // CH
LEVELS = 7
DFF = 2816
FT = DFF // P
GROUPS = [(0, 8), (8, 7), (15, 7)]
EPS = 1e-6
NEG = -1e30
TINY = 2.0 ** -64

PER_IT = 14
U_TAIL = HEADS * PER_IT
U_C = U_TAIL + 4
U_D = U_C + KT
U_E = U_D + KT
U_F = U_E + KT
U_G = U_F + KT
UNITS = U_G + 2 * FT + len(GROUPS) * KT

C_MASK, C_RESET, C_NEGTRI, C_NEGREST, C_SMASK, C_NEGM, C_ONES, C_IDENT = 0, 1024, 2048, 2176, 2304, 2432, 2560, 2688
C_ALL = 2816
V_MIX, V_XATTN, V_MEM, V_FFN, V_FINAL, V_HGRN, V_LB0, V_LB1, V_EPS = 0, 8, 16, 24, 32, 40, 44, 48, 52
V_ALL = 56

SB_STEPS = [(0, j) for j in range(3, -1, -1)] + [(1, j) for j in range(7, -1, -1)]
SB_N = len(SB_STEPS)


def constants():
    c = np.zeros((P, C_ALL), np.float32)
    s, t = np.arange(P)[:, None], np.arange(P)[None, :]
    for lev in range(LEVELS):
        m = CH >> (lev + 1)
        pair = (s // (2 * m) == t // (2 * m)) & (s % (2 * m) < m) & (t % (2 * m) >= m)
        c[:, C_MASK + lev * P:C_MASK + (lev + 1) * P] = pair
    c[:, C_MASK + LEVELS * P:C_MASK + (LEVELS + 1) * P] = s == t
    c[:, C_RESET:C_RESET + T] = (np.arange(T) % CH != 0)[None, :]
    c[:, C_NEGTRI:C_NEGTRI + P] = -1.0 * (s >= t)
    c[:, C_NEGREST:C_NEGREST + P] = -1.0 * (s < t)
    c[:, C_SMASK:C_SMASK + P] = s < t
    c[:, C_NEGM:C_NEGM + P] = NEG * (s >= t)
    c[:, C_ONES:C_ONES + P] = 1.0
    c[:, C_IDENT:C_IDENT + P] = s == t
    return c


SEMS = """
cst_in vec_in mem_in x_in raw0_in raw1_in
w_hi_made weights_ready unit_done pair_free dve_seq
lb_diff lb_exp consts_cast prep_dve prep_act prep_pe sqm_used sq0_used h_ready
hgrn_exp hgrn_f hgrn_lf
iT_done vtok_copied at_zero d_ready e_ready qk_ready s_done pred_done
qe_ready ke_ready keT_done keT_copied u_done state_ready o_done osq_ready hms_done hln hr_ready
y_f32 y_hi_done y_lo_done y_stored
kq_hi kq_lo vT_done v_hi v_lo
z_done z_copied nu_done ex_done ln_done sp_pre sp_done sph_done spl_done cum1_done la_pre la_done cum2_done
a_done ah_done al_done av_done yb_f32 yb_hi yb_lo yb_stored
out0_stored out1_stored tail_stored y_loaded
ga0_in ga1_in gb0_in gb1_in gates_sig t1_done m_done c_hi c_lo
old0_in old1_in new0_stored new1_stored g_hi g_lo sq_done sq_acc sqz norm_pe norm_sqrt r_ready
kv_in vtokE_pe vtokE_done s_ready mx_done nmx_done p_exp p_rec p_done pT_pe pT_done oE_pe oE_hi oE_lo
f_silu f_prod f_hi f_lo final_done stored
""".split()


def build(nc, xT, memT, vecs, cst, weights, out):
    ctx = ExitStack()
    with ctx:
        sem = {n: ctx.enter_context(nc.semaphore(n)) for n in SEMS}

        base = (nc.sbuf_base + 31) // 32 * 32
        K = 1024

        def at(name, offset, shape, dt=F32):
            return nc.alloc_sbuf_tensor_at(name, shape, dt, offset=base + int(offset))

        A0, W0 = 0, 64 * K
        X0, T0 = W0 + 64 * K, W0 + 96 * K
        RING, R0, S0 = W0 + 112 * K, W0 + 136 * K, W0 + 140 * K
        A_hi, A_lo = at("A_hi", A0, [P, KT, T], F32R), at("A_lo", A0 + 32 * K, [P, KT, T], F32R)
        B_hi, B_lo = at("B_hi", W0, [P, KT, T], F32R), at("B_lo", W0 + 32 * K, [P, KT, T], F32R)
        X = at("X", X0, [P, KT, T])
        raw = at("raw", RING, [P, 2, D])
        w_hi = at("w_hi", RING + 8 * K, [P, 2, D], F32R)
        w_lo = at("w_lo", RING + 16 * K, [P, 2, D], F32R)
        R = at("R", R0, [P, T])
        vec = at("vec", S0, [P, V_ALL])
        lb = at("lb", S0 + 256, [P, 4, 4])
        ones = at("ones", S0 + 512, [P, P])
        ident = at("ident", S0 + 1024, [P, P])
        stat = at("stat", S0 + 1536, [P, 4, 4])

        mask = at("mask", W0, [P, LEVELS + 1, P])
        reset = at("reset", W0 + 4 * K, [P, T])
        qf, kf, vf = (at(n, W0 + (8 + 4 * i) * K, [P, T]) for i, n in enumerate(("qf", "kf", "vf")))
        outr = at("outr", W0 + 20 * K, [P, 2, T])
        M_hi, M_lo = at("M_hi", W0 + 28 * K, [P, KT, M], F32R), at("M_lo", W0 + 36 * K, [P, KT, M], F32R)
        U0 = W0 + 44 * K
        Rm = at("Rm", W0 + 108 * K, [P, M])
        negtri = at("negtri", W0 + 109 * K, [P, P], F32R)
        negrest = at("negrest", W0 + 109 * K + 512, [P, P], F32R)
        smask = at("smask", W0 + 110 * K, [P, P])
        negm = at("negm", W0 + 110 * K + 512, [P, P])
        fq, iv, qh, og, kk, bb = (at(n, U0 + o * K, [P, T]) for n, o in
                                  (("fq", 0), ("iv", 4), ("qh", 8), ("og", 12), ("kk", 16), ("bb", 20)))
        Dl = [fq, iv]
        vtok = at("vtok", U0 + 24 * K, [P, NCH, P])
        AT = at("AT", U0 + 28 * K, [P, NCH, P])
        Qe, Ke = at("Qe", U0 + 32 * K, [P, T]), at("Ke", U0 + 36 * K, [P, T])
        Ketok = at("Ketok", U0 + 40 * K, [P, NCH, P])
        St = at("St", U0 + 44 * K, [P, NCH, P])
        QK = [at(f"QK{i}", U0 + (48 + 4 * i) * K, [P, T]) for i in range(2)]
        El = [at(f"El{i}", U0 + (56 + 4 * i) * K, [P, T]) for i in range(2)]
        ya_hi, ya_lo = at("ya_hi", U0 + 56 * K, [P, T], F32R), at("ya_lo", U0 + 60 * K, [P, T], F32R)
        K2 = at("K2", U0, [P, 2, T], F32R)
        Q2h, Q2l = at("Q2h", U0 + 8 * K, [P, 2, T], F32R), at("Q2l", U0 + 16 * K, [P, 2, T], F32R)
        V2 = at("V2", U0 + 24 * K, [P, NCH, 2, P], F32R)
        zs = [at(f"zs{i}", U0 + (32 + 4 * i) * K, [P, 2, HALF]) for i in range(2)]
        el = [at(f"el{i}", U0 + (40 + 4 * i) * K, [P, 2, HALF]) for i in range(2)]
        sph, spl, ah, al = (at(n, U0 + (48 + 4 * i) * K, [P, 2, HALF], F32R)
                            for i, n in enumerate(("sph", "spl", "ah", "al")))
        yb_hi, yb_lo = at("yb_hi", W0 + 8 * K, [P, T], F32R), at("yb_lo", W0 + 12 * K, [P, T], F32R)
        ybf = at("ybf", W0 + 16 * K, [P, HALF])
        x0 = at("x0", U0, [P, KT, T])
        sq0, SQ0 = at("sq0", U0 + 32 * K, [P, T]), at("SQ0", U0 + 36 * K, [P, T])
        mem0 = at("mem0", U0 + 40 * K, [P, KT, M])
        sqm, SQm = at("sqm", U0 + 48 * K, [P, M]), at("SQm", U0 + 49 * K, [P, M])
        tri0 = at("tri0", U0 + 50 * K, [P, 2, P])
        ga = [at(f"ga{i}", X0 + 4 * i * K, [P, T]) for i in range(2)]
        gb = [at(f"gb{i}", X0 + (8 + 4 * i) * K, [P, T]) for i in range(2)]
        t1 = [at(f"t1{i}", X0 + (16 + 4 * i) * K, [P, T]) for i in range(2)]
        t2 = [at(f"t2{i}", X0 + (24 + 4 * i) * K, [P, T]) for i in range(2)]
        tail = t1 + t2
        old = [at(f"old{i}", T0 + 4 * i * K, [P, T]) for i in range(2)]
        sq, SQ = at("sq", T0 + 8 * K, [P, T]), at("SQ", T0 + 12 * K, [P, T])
        new = [at(f"new{i}", X0 + 4 * i * K, [P, T]) for i in range(2)]
        qx = at("qx", X0, [P, 2, T])
        kx = at("kx", X0 + 8 * K, [P, 2, M])
        vx = at("vx", X0 + 10 * K, [P, 2, M])
        vxt = at("vxt", X0 + 12 * K, [P, 2, M])
        px = at("px", X0 + 14 * K, [P, 4, M])
        pxT = at("pxT", X0 + 18 * K, [P, 2, HALF])
        gt, ut = at("gt", T0, [P, T]), at("ut", T0 + 4 * K, [P, T])

        ps = ctx.enter_context(nc.psum_tensor("ps", [P, 8, HALF], F32))

        def wide(b):
            return ps[:, b:b + 2, :].rearrange("p a b -> p (a b)")

        gate_d = nc.dram_tensor("gate_d", [16, P, T], F32).ap()
        kv_d = nc.dram_tensor("kv_d", [16, P, M], F32).ap()
        y_d = nc.dram_tensor("y_d", [2, 8, P, T], F32).ap()
        x1_d = nc.dram_tensor("x1_d", [KT, P, T], F32).ap()

        def row(t, i):
            return t[bass.ds(i, 1)].rearrange("o p n -> p (o n)")

        block = ctx.enter_context(nc.Block())
        raw_in = [sem["raw0_in"], sem["raw1_in"]]
        out_stored = [sem["out0_stored"], sem["out1_stored"]]
        new_stored = [sem["new0_stored"], sem["new1_stored"]]
        old_in = [sem["old0_in"], sem["old1_in"]]
        ga_in, gb_in = [sem["ga0_in"], sem["ga1_in"]], [sem["gb0_in"], sem["gb1_in"]]

        @block.sync
        def _(sp):
            sp.dma_start(vec[:], vecs).then_inc(sem["vec_in"], 16)
            sp.dma_start(mem0[:], memT).then_inc(sem["mem_in"], 16)
            for s in range(2):
                sp.dma_start(raw[:, s], weights[s]).then_inc(raw_in[s], 16)
            sp.dma_start(x0[:], xT).then_inc(sem["x_in"], 16)
            with sp.Fori(1, UNITS // 2) as p:
                for s in range(2):
                    sp.wait_ge(sem["weights_ready"], p * 2 + (s - 1))
                    sp.dma_start(raw[:, s], row(weights, p * 2 + s)).then_inc(raw_in[s], 16)

        @block.gpsimd
        def _(pool):
            def split(u, s, n, first):
                pool.wait_ge(raw_in[s], n * 16 + 16)
                if not first:
                    pool.wait_ge(sem["unit_done"], u - 1)
                pool.nop(nofuse=True)
                pool.tensor_copy(w_hi[:, s], raw[:, s]).then_inc(sem["w_hi_made"], 1)
                pool.wait_ge(sem["w_hi_made"], u + 1)
                pool.tensor_tensor(w_lo[:, s], raw[:, s], w_hi[:, s].bitcast(F32),
                                   ALU.subtract).then_inc(sem["weights_ready"], 1)

            for s in range(2):
                split(s, s, 0, True)
            with pool.Fori(1, UNITS // 2) as p:
                for s in range(2):
                    split(p * 2 + s, s, p, False)

        @block.tensor
        def _(pe):
            def k_steps(u, s, hi, lo, dest, k0, k1, kts=KT, kb=0, last=True):
                for k in range(k0, k1):
                    wh, wl = (w[:, s, (kb + k) * P:(kb + k + 1) * P] for w in (w_hi, w_lo))
                    for n, (w, a) in enumerate(((wh, hi), (wh, lo), (wl, hi))):
                        for c, (bank, cols) in enumerate(dest):
                            mm = pe.matmul(bank, w, a[:, k, cols], start=(k == 0 and n == 0),
                                           stop=(k == kts - 1 and n == 2), skip_group_check=True)
                if k1 == kts and last:
                    mm.then_inc(sem["unit_done"], 1)

            def halves(b):
                return [(ps[:, b, :], slice(0, HALF)), (ps[:, b + 1, :], slice(HALF, T))]

            def begin(u, only_pair=False):
                pe.wait_ge(sem["weights_ready"], u + 1)
                pe.wait_ge(sem["pair_free"], u + (2 if only_pair else 1))

            def unit(u, s, hi, lo, b, only_pair=False, kts=KT):
                begin(u, only_pair)
                k_steps(u, s, hi, lo, halves(b), 0, kts, kts=kts)

            def norm_sum(acc, cols, b):
                n = min(cols, HALF)
                for c in range(cols // n):
                    mm = pe.matmul(ps[:, b + c, 0:n], ones[:], acc[:, c * n:(c + 1) * n], start=True, stop=True)
                return mm

            pe.wait_ge(sem["cst_in"], 7 * 16)
            pe.wait_ge(sem["prep_dve"], 1)
            norm_sum(SQm, M, 4).then_inc(sem["prep_pe"], 1)
            pe.wait_ge(sem["prep_dve"], 2)
            pe.wait_ge(sem["norm_sqrt"], 1)
            norm_sum(SQ0, T, 4).then_inc(sem["prep_pe"], 1)
            pe.wait_ge(sem["h_ready"], 1)
            pe.wait_ge(sem["consts_cast"], 1)

            with pe.Fori(0, HEADS) as it:
                U = it * PER_IT
                unit(U, 0, A_hi, A_lo, 0, only_pair=True)
                pe.wait_ge(sem["z_copied"], it * SB_N + 1)
                unit(U + 1, 1, A_hi, A_lo, 2)
                unit(U + 2, 0, A_hi, A_lo, 0)
                unit(U + 3, 1, A_hi, A_lo, 2)

                pe.wait_ge(sem["pair_free"], U + 5)
                for c in range(NCH):
                    mm = pe.transpose(ps[:, 4 + c // 4, (c % 4) * P:(c % 4 + 1) * P], iv[:, c * P:(c + 1) * P], ident[:])
                mm.then_inc(sem["iT_done"], 1)

                def fill_qkv(i):
                    for n in range(3 * i, 3 * i + 3):
                        w, k = n // KT, n % KT
                        if k == 0:
                            begin(U + 4 + w)
                        k_steps(U + 4 + w, w % 2, A_hi, A_lo, halves(2 * (w % 2)), k, k + 1)

                for lev in range(LEVELS + 1):
                    b = 4 + 2 * ((lev + 1) % 2)
                    if lev < LEVELS:
                        pe.wait_ge(sem["qk_ready"], it * LEVELS + lev + 1)
                        ks = qs = QK[lev % 2]
                    else:
                        ks, qs = kk, qh
                    if lev == 1:
                        pe.wait_ge(sem["vtok_copied"], it + 1)
                    elif lev >= 2:
                        pe.wait_ge(sem["pred_done"], it * (LEVELS + 1) + lev - 1)
                    for c in range(NCH):
                        mm = pe.matmul(ps[:, b + c // 4, (c % 4) * P:(c % 4 + 1) * P],
                                       ks[:, c * P:(c + 1) * P], qs[:, c * P:(c + 1) * P], start=True, stop=True)
                    mm.then_inc(sem["s_done"], 1)
                    fill_qkv(lev)

                pe.wait_ge(sem["ke_ready"], it + 1)
                pe.wait_ge(sem["pred_done"], it * (LEVELS + 1) + LEVELS)
                for c in range(NCH):
                    mm = pe.transpose(ps[:, 6 + c // 4, (c % 4) * P:(c % 4 + 1) * P], Ke[:, c * P:(c + 1) * P], ident[:])
                mm.then_inc(sem["keT_done"], 1)
                pe.wait_ge(sem["keT_copied"], it + 1)
                pe.wait_ge(sem["pred_done"], it * (LEVELS + 1) + LEVELS + 1)
                for c in range(NCH - 1):
                    mm = pe.matmul(ps[:, 4 + c // 4, (c % 4) * P:(c % 4 + 1) * P], Ketok[:, c, :], vtok[:, c, :],
                                   start=True, stop=True)
                mm.then_inc(sem["u_done"], 1)
                for c in range(NCH):
                    o = ps[:, 6 + c // 4, (c % 4) * P:(c % 4 + 1) * P]
                    mm = pe.matmul(o, vtok[:, c, :], AT[:, c, :], start=True, stop=(c == 0))
                    if c:
                        pe.wait_ge(sem["state_ready"], it * (NCH - 1) + c)
                        mm = pe.matmul(o, St[:, c, :], Qe[:, c * P:(c + 1) * P], start=False, stop=True)
                mm.then_inc(sem["o_done"], 1)
                pe.wait_ge(sem["osq_ready"], it + 1)
                norm_sum(QK[1], T, 4).then_inc(sem["hms_done"], 1)

                pe.wait_ge(sem["pair_free"], U + 9)
                pe.wait_ge(sem["hr_ready"], it + 1)
                for c in range(NCH):
                    mm = pe.transpose(ps[:, 4 + c // 4, (c % 4) * P:(c % 4 + 1) * P], vf[:, c * P:(c + 1) * P], ident[:])
                mm.then_inc(sem["vT_done"], 1)
                pe.wait_ge(sem["kq_lo"], it + 1)

                def cols(s):
                    c, j = SB_STEPS[s]
                    return max(0, j * P - c * HALF)

                def scores(s):
                    c, j = SB_STEPS[s]
                    g = it * SB_N + s
                    if s:
                        pe.wait_ge(sem["z_copied"], g + 1)
                    for a in range(2):
                        for n, q in enumerate((Q2h, Q2l)):
                            mm = pe.matmul(ps[:, 2 + a, cols(s):HALF], K2[:, a, j * P:(j + 1) * P],
                                           q[:, a, c * HALF + cols(s):(c + 1) * HALF], start=(n == 0), stop=(n == 1))
                    mm.then_inc(sem["z_done"], 1)

                def cumulate(s, sel, name, first):
                    for a in range(2):
                        for n, x in enumerate((sph, spl)):
                            mm = pe.matmul(ps[:, 4 + a, cols(s):HALF], sel[:], x[:, a, cols(s):HALF],
                                           start=(first and n == 0), stop=True, skip_group_check=True)
                    mm.then_inc(sem[name], 1)

                def values(s):
                    c, j = SB_STEPS[s]
                    pe.wait_ge(sem["al_done"], it * SB_N + s + 1)
                    if s == 4:
                        pe.wait_ge(sem["yb_f32"], it * 4 + 2)
                    for a in range(2):
                        for n, x in enumerate((ah, al)):
                            mm = pe.matmul(ps[:, 6 + a, cols(s):HALF], V2[:, j, a, :], x[:, a, cols(s):HALF],
                                           start=(s in (0, 4) and n == 0), stop=True, skip_group_check=True)
                    mm.then_inc(sem["av_done"], 1)

                def fill_gates(s):
                    if s < 9:
                        w = 7 + s // 3
                        k0, k1 = ((0, 3), (3, 6), (6, 8))[s % 3]
                        if k0 == 0:
                            begin(U + w, only_pair=True)
                        k_steps(U + w, w % 2, A_hi, A_lo, halves(0), k0, k1)
                    else:
                        for w in {9: (10, 11), 10: (12,), 11: (13,)}[s]:
                            begin(U + w, only_pair=(w == 10))
                            k_steps(U + w, w % 2, M_hi, M_lo, [(ps[:, w % 2, 0:M], slice(0, M))], 0, KT)

                pe.wait_ge(sem["v_lo"], it + 1)
                scores(0)
                n2 = 0
                for s in range(SB_N):
                    g = it * SB_N + s
                    first = s in (0, 4)
                    if s + 1 < SB_N:
                        scores(s + 1)
                    fill_gates(s)
                    pe.wait_ge(sem["spl_done"], g + 1)
                    if first and s:
                        pe.wait_ge(sem["la_done"], g)
                    cumulate(s, negtri, "cum1_done", first)
                    if s:
                        values(s - 1)
                    if SB_STEPS[s][1]:
                        pe.wait_ge(sem["la_done"], g + 1)
                        cumulate(s, negrest, "cum2_done", False)
                values(SB_N - 1)

            for w in range(4):
                unit(U_TAIL + w, w % 2, A_hi, A_lo, 2 * (w % 2), only_pair=(w == 0))
            pe.wait_ge(sem["y_loaded"], 32)
            pe.wait_ge(sem["pair_free"], U_C + 2)
            with pe.Fori(0, KT // 2) as p:
                for s in range(2):
                    u = p * 2 + (U_C + s)
                    begin(u)
                    k_steps(u, s, B_hi, B_lo, halves(4 * s), 0, 4, kts=4, last=False)
                    k_steps(u, s, B_hi[:, 4:8, :], B_lo[:, 4:8, :], halves(4 * s + 2), 0, 4, kts=4, kb=4)

            def linear(u0, hi, lo, first_wait):
                pe.wait_ge(*first_wait)
                with pe.Fori(0, KT // 2) as p:
                    for s in range(2):
                        unit(p * 2 + (u0 + s), s, hi, lo, 2 * s)

            def norm_of(n):
                pe.wait_ge(sem["sq_acc"], n * KT + 1)
                norm_sum(SQ, T, 4).then_inc(sem["norm_pe"], 1)

            pe.wait_ge(sem["pair_free"], U_C + KT + 2)
            linear(U_D, A_hi, A_lo, (sem["c_lo"], KT))
            norm_of(1)
            pe.wait_ge(sem["g_lo"], KT)
            with pe.Fori(0, HEADS) as h:
                for s in range(2):
                    unit(h * 2 + (U_E + s), s, B_hi, B_lo, 2 * s)
                pe.wait_ge(sem["kv_in"], h * 32 + 32)
                pe.wait_ge(sem["r_ready"], 1)
                pe.wait_ge(sem["oE_lo"], h * 2 + 1)
                for ds in range(2):
                    for mt in range(2):
                        mm = pe.transpose(ps[:, 6, mt * M + ds * P:mt * M + (ds + 1) * P],
                                          vx[:, ds, mt * P:(mt + 1) * P], ident[:])
                mm.then_inc(sem["vtokE_pe"], 1)
                pe.wait_ge(sem["pair_free"], h * 2 + (U_E + 4))
                for hf in range(2):
                    pe.wait_ge(sem["oE_lo"], h * 2 + (hf + 1))
                    for tt in range(4):
                        for ds in range(2):
                            t = hf * HALF + tt * P
                            mm = pe.matmul(ps[:, 4 + tt // 2, (tt % 2) * M:(tt % 2 + 1) * M], qx[:, ds, t:t + P],
                                           kx[:, ds, :], start=(ds == 0), stop=(ds == 1))
                    mm.then_inc(sem["s_ready"], 1)
                    pe.wait_ge(sem["p_done"], h * 2 + (hf + 1))
                    pe.wait_ge(sem["vtokE_done"], h + 1)
                    for tt in range(4):
                        for mt in range(2):
                            mm = pe.transpose(ps[:, 6 + mt, tt * P:(tt + 1) * P], px[:, tt, mt * P:(mt + 1) * P], ident[:])
                    mm.then_inc(sem["pT_pe"], 1)
                    pe.wait_ge(sem["pT_done"], h * 2 + (hf + 1))
                    for ds in range(2):
                        for mt in range(2):
                            mm = pe.matmul(ps[:, 4 + ds, :], vxt[:, mt, ds * P:(ds + 1) * P], pxT[:, mt, :],
                                           start=(mt == 0), stop=(mt == 1))
                    mm.then_inc(sem["oE_pe"], 1)
            linear(U_F, A_hi, A_lo, (sem["oE_lo"], 2 * HEADS + 1))
            norm_of(2)
            pe.wait_ge(sem["g_lo"], 2 * KT)
            u0 = U_G
            for f0, nf in GROUPS:
                with pe.Fori(0, nf) as f:
                    for s in range(2):
                        unit(f * 2 + (u0 + s), s, B_hi, B_lo, 2 * s)
                pe.wait_ge(sem["f_lo"], f0 + nf + 1)
                with pe.Fori(0, KT // 2) as p:
                    for s in range(2):
                        unit(p * 2 + (u0 + 2 * nf + s), s, A_hi, A_lo, 2 * s, kts=nf)
                u0 += 2 * nf + KT
            norm_of(3)

        @block.vector
        def _(dve):
            seq = {"base": 0, "n": 0}

            def link(ins):
                seq["n"] += 1
                ins.then_inc(sem["dve_seq"], 1)
                dve.wait_ge(sem["dve_seq"], seq["base"] + seq["n"])

            def scaled(dst, src, r):
                return dve.tensor_tensor(dst, src, r, ALU.mult)

            dve.sem_inc(sem["pair_free"], 2)
            dve.sem_inc(sem["sq_acc"], 1)
            dve.sem_inc(sem["f_lo"], 1)
            dve.wait_ge(sem["vec_in"], 16)
            dve.wait_ge(sem["cst_in"], 7 * 16)
            l0, l1 = vec[:, V_LB0:V_LB0 + 4], vec[:, V_LB1:V_LB1 + 4]
            link(dve.tensor_tensor(lb[:, 0], l0, l1, ALU.max))
            link(dve.tensor_tensor(lb[:, 1], l0, lb[:, 0], ALU.subtract))
            dve.tensor_tensor(lb[:, 2], l1, lb[:, 0], ALU.subtract).then_inc(sem["lb_diff"], 1)
            dve.wait_ge(sem["lb_exp"], 2)
            link(dve.tensor_tensor(lb[:, 0], lb[:, 1], lb[:, 2], ALU.add))
            link(dve.reciprocal(lb[:, 3], lb[:, 0]))
            link(dve.tensor_tensor(lb[:, 0], lb[:, 1], lb[:, 3], ALU.mult))
            link(dve.tensor_tensor(lb[:, 1], lb[:, 2], lb[:, 3], ALU.mult))

            def split_norm(src, g, hi, lo, tmp, acc, act_n, used):
                for k in range(KT):
                    dve.wait_ge(sem["prep_act"], act_n + 2 * k + 1)
                    dve.scalar_tensor_tensor(lo[:, k], src[:, k], vec[:, g + k:g + k + 1], hi[:, k].bitcast(F32),
                                             ALU.mult, ALU.subtract)
                    dve.wait_ge(sem["prep_act"], act_n + 2 * k + 2)
                    if k == 0:
                        op = dve.tensor_copy(acc[:], tmp[:])
                    else:
                        op = dve.tensor_tensor(acc[:], acc[:], tmp[:], ALU.add)
                    op.then_inc(used, 1)
                    dve.wait_ge(used, k + 1)
                dve.sem_inc(sem["prep_dve"], 1)

            split_norm(mem0, V_MEM, M_hi, M_lo, sqm, SQm, 0, sem["sqm_used"])
            split_norm(x0, V_MIX, A_hi, A_lo, sq0, SQ0, 2 * KT, sem["sq0_used"])
            dve.wait_ge(sem["norm_sqrt"], 1)
            link(dve.reciprocal(Rm[:], sqm[:]))
            dve.wait_ge(sem["norm_sqrt"], 2)
            link(dve.reciprocal(R[:], sq0[:]))
            dve.sem_inc(sem["h_ready"], 1)

            seq0 = seq["n"]
            seq["n"] = 0
            LINKS = 12
            with dve.Fori(0, HEADS) as it:
                seq["base"] = it * LINKS + seq0
                U = it * PER_IT

                def leave(i, dst, b, r=R):
                    dve.wait_ge(sem["unit_done"], U + i + 1)
                    scaled(dst, b, r[:]).then_inc(sem["pair_free"], 1)

                leave(0, fq[:], wide(0))
                leave(1, qh[:], wide(2))
                leave(2, iv[:], wide(0))
                leave(3, og[:], wide(2))
                dve.wait_ge(sem["hgrn_exp"], it * 3 + 1)
                link(dve.tensor_scalar(bb[:], El[0][:], 1.0, None, ALU.add))
                link(dve.reciprocal(kk[:], bb[:]))
                link(dve.tensor_scalar(El[0][:], kk[:], lb[:, 1, bass.ds(it, 1)], lb[:, 0, bass.ds(it, 1)], ALU.mult, ALU.add))
                dve.tensor_scalar(kk[:], El[0][:], -1.0, 1.0, ALU.mult, ALU.add)
                dve.tensor_scalar(bb[:], El[0][:], TINY, None, ALU.max).then_inc(sem["hgrn_f"], 1)
                dve.wait_ge(sem["hgrn_exp"], it * 3 + 2)
                link(dve.tensor_scalar(El[1][:], El[1][:], 1.0, None, ALU.add))
                link(dve.reciprocal(El[1][:], El[1][:]))
                dve.tensor_tensor(qh[:], qh[:], El[1][:], ALU.mult)
                dve.wait_ge(sem["hgrn_exp"], it * 3 + 3)
                link(dve.tensor_scalar(QK[0][:], QK[0][:], 1.0, None, ALU.add))
                link(dve.reciprocal(QK[0][:], QK[0][:]))
                dve.tensor_tensor(og[:], og[:], QK[0][:], ALU.mult)
                dve.wait_ge(sem["hgrn_lf"], it + 1)
                link(dve.tensor_tensor_scan(bb[:], reset[:], QK[1][:], 0.0, ALU.mult, ALU.add))
                dve.memset(AT[:], 0.0).then_inc(sem["at_zero"], 1)

                def diff(lev):
                    m = CH >> (lev + 1)
                    b3 = bb[:].rearrange("p (n w) -> p n w", w=2 * m)
                    d3 = Dl[lev % 2][:].rearrange("p (n w) -> p n w", w=2 * m)
                    n = T // (2 * m)
                    if lev == 1:
                        dve.wait_ge(sem["iT_done"], it + 1)
                    dve.tensor_tensor(d3, b3, b3[:, :, m - 1:m].broadcast_to([P, n, 2 * m]), ALU.subtract)\
                       .then_inc(sem["d_ready"], 1)

                def weigh(lev):
                    m = CH >> (lev + 1)
                    dve.wait_ge(sem["e_ready"], it * 9 + lev + 1)
                    if lev >= 2:
                        dve.wait_ge(sem["s_done"], it * (LEVELS + 1) + lev - 1)
                    e, k, q, o = (x[:].rearrange("p (n h m) -> p n h m", h=2, m=m) for x in (El[lev % 2], kk, qh, QK[lev % 2]))
                    dve.tensor_tensor(o[:, :, 0], e[:, :, 0], k[:, :, 0], ALU.mult)
                    dve.tensor_tensor(o[:, :, 1], e[:, :, 1], q[:, :, 1], ALU.mult).then_inc(sem["qk_ready"], 1)

                def pick(lev):
                    b = 4 + 2 * ((lev + 1) % 2)
                    dve.wait_ge(sem["s_done"], it * (LEVELS + 1) + lev + 1)
                    if lev:
                        dve.wait_ge(sem["pred_done"], it * (LEVELS + 1) + lev)
                    else:
                        dve.wait_ge(sem["at_zero"], it + 1)
                    dve.nop(nofuse=True)
                    dve.copy_predicated(AT[:], mask[:, lev, :].bitcast(I32).unsqueeze(1).broadcast_to([P, NCH, P]),
                                        ps[:, b:b + 2, :].rearrange("p a (c t) -> p (a c) t", t=P)).then_inc(sem["pred_done"], 1)

                diff(0)
                diff(1)
                weigh(0)
                for lev in range(1, LEVELS):
                    if lev + 1 < LEVELS:
                        diff(lev + 1)
                    weigh(lev)
                    pick(lev - 1)
                    if lev == 4:
                        dve.wait_ge(sem["yb_stored"], it * 32 + 32)
                        dve.wait_ge(sem["unit_done"], U + 5)
                        dve.scalar_tensor_tensor(qf[:], wide(0), 0.125, R[:], ALU.mult, ALU.mult).then_inc(sem["pair_free"], 1)
                b3 = bb[:].rearrange("p (n w) -> p n w", w=CH)
                dve.tensor_tensor(Dl[0][:].rearrange("p (n w) -> p n w", w=CH), b3[:, :, CH - 1:CH].broadcast_to([P, NCH, CH]),
                                  b3, ALU.subtract).then_inc(sem["d_ready"], 1)
                dve.wait_ge(sem["e_ready"], it * 9 + 8)
                dve.tensor_tensor(Qe[:], qh[:], El[1][:], ALU.mult).then_inc(sem["qe_ready"], 1)
                dve.wait_ge(sem["e_ready"], it * 9 + 9)
                dve.tensor_tensor(Ke[:], kk[:], El[0][:], ALU.mult).then_inc(sem["ke_ready"], 1)
                pick(LEVELS - 1)
                leave(5, kf[:], wide(2))
                pick(LEVELS)
                leave(6, vf[:], wide(0))
                dve.wait_ge(sem["u_done"], it + 1)
                for c in range(1, NCH):
                    u = ps[:, 4 + (c - 1) // 4, ((c - 1) % 4) * P:((c - 1) % 4 + 1) * P]
                    if c == 1:
                        dve.tensor_copy(St[:, 1, :], u).then_inc(sem["state_ready"], 1)
                    else:
                        dve.wait_ge(sem["state_ready"], it * (NCH - 1) + c - 1)
                        dve.scalar_tensor_tensor(St[:, c, :], St[:, c - 1, :], El[1][:, c * P - 1:c * P], u,
                                                 ALU.mult, ALU.add).then_inc(sem["state_ready"], 1)
                dve.wait_ge(sem["hr_ready"], it + 1)
                link(dve.scalar_tensor_tensor(QK[0][:], QK[0][:], vec[:, bass.ds(it + V_HGRN, 1)], fq[:], ALU.mult, ALU.mult))
                link(dve.tensor_tensor(QK[0][:], QK[0][:], og[:], ALU.mult))
                dve.sem_inc(sem["y_f32"], 1)
                dve.wait_ge(sem["y_hi_done"], it + 1)
                dve.tensor_tensor(ya_lo[:], QK[0][:], ya_hi[:].bitcast(F32), ALU.subtract).then_inc(sem["y_lo_done"], 1)

                dve.wait_ge(sem["kq_hi"], it * 6 + 6)
                lo_of = lambda dst, src, hi: dve.tensor_tensor(dst, src, hi.bitcast(F32), ALU.subtract)
                h0, h1 = slice(0, 64), slice(64, 128)
                lo_of(K2[h1, 0], kf[h0], K2[h0, 0])
                lo_of(K2[h0, 1], kf[h1], K2[h1, 1])
                lo_of(Q2l[h0, 0], qf[h0], Q2h[h0, 0])
                lo_of(Q2l[h1, 0], qf[h0], Q2h[h0, 0])
                lo_of(Q2l[h0, 1], qf[h1], Q2h[h1, 1])
                lo_of(Q2l[h1, 1], qf[h1], Q2h[h1, 1]).then_inc(sem["kq_lo"], 1)
                dve.wait_ge(sem["v_hi"], it + 1)
                vps = ps[:, 4:6, :].rearrange("p a (c h d) -> p (a c) h d", h=2, d=64)
                dve.tensor_tensor(V2[:, :, :, 64:128], vps, V2[:, :, :, 0:64].bitcast(F32), ALU.subtract).then_inc(sem["v_lo"], 1)

                def cols(s):
                    c, j = SB_STEPS[s]
                    return max(0, j * P - c * HALF)

                def diagonal(s):
                    c, j = SB_STEPS[s]
                    return j * P >= c * HALF

                n_diag = sum(diagonal(s) for s in range(SB_N))

                def neg_abs(s):
                    g = it * SB_N + s
                    dve.wait_ge(sem["z_copied"], g + 2)
                    z = zs[s % 2][:, :, cols(s):]
                    dve.scalar_tensor_tensor(el[s % 2][:, :, cols(s):], z, -1.0, z, ALU.mult, ALU.min).then_inc(sem["nu_done"], 1)

                def softplus(s):
                    g = it * SB_N + s
                    dve.wait_ge(sem["ln_done"], g + 1)
                    e = el[s % 2][:, :, cols(s):]
                    op = dve.scalar_tensor_tensor(e, zs[s % 2][:, :, cols(s):], 0.0, e, ALU.max, ALU.add)
                    if diagonal(s):
                        nd = sum(diagonal(x) for x in range(s))
                        op.then_inc(sem["sp_pre"], 1)
                        dve.wait_ge(sem["sp_pre"], it * n_diag + nd + 1)
                        e = el[s % 2][:, :, cols(s):cols(s) + P]
                        op = dve.tensor_tensor(e, e, smask[:].unsqueeze(1).broadcast_to([P, 2, P]), ALU.mult)
                    op.then_inc(sem["sp_done"], 1)

                def softplus_lo(s):
                    dve.wait_ge(sem["sph_done"], it * SB_N + s + 1)
                    dve.tensor_tensor(spl[:, :, cols(s):], el[s % 2][:, :, cols(s):], sph[:, :, cols(s):].bitcast(F32),
                                      ALU.subtract).then_inc(sem["spl_done"], 1)

                def log_a(s):
                    g = it * SB_N + s
                    dve.wait_ge(sem["cum1_done"], g + 1)
                    z = zs[s % 2][:, :, cols(s):]
                    op = dve.tensor_tensor(z, z, ps[:, 4:6, cols(s):HALF], ALU.add)
                    if diagonal(s):
                        nd = sum(diagonal(x) for x in range(s))
                        op.then_inc(sem["la_pre"], 1)
                        dve.wait_ge(sem["la_pre"], it * n_diag + nd + 1)
                        z = zs[s % 2][:, :, cols(s):cols(s) + P]
                        op = dve.tensor_tensor(z, z, negm[:].unsqueeze(1).broadcast_to([P, 2, P]), ALU.add)
                    op.then_inc(sem["la_done"], 1)

                def a_lo(s):
                    dve.wait_ge(sem["ah_done"], it * SB_N + s + 1)
                    dve.tensor_tensor(al[:, :, cols(s):], zs[s % 2][:, :, cols(s):], ah[:, :, cols(s):].bitcast(F32),
                                      ALU.subtract).then_inc(sem["al_done"], 1)

                def leave_o(s, c):
                    dve.wait_ge(sem["av_done"], it * SB_N + s + 1)
                    dve.tensor_copy(ybf[0:64], ps[64:128, 6, :])
                    link(dve.tensor_copy(ybf[64:128], ps[64:128, 7, :]))
                    dve.tensor_tensor(ybf[0:64], ps[0:64, 6, :], ybf[0:64], ALU.add).then_inc(sem["yb_f32"], 1)
                    dve.tensor_tensor(ybf[64:128], ps[0:64, 7, :], ybf[64:128], ALU.add).then_inc(sem["yb_f32"], 1)
                    dve.wait_ge(sem["yb_hi"], it * 2 + c + 1)
                    cc = slice(c * HALF, (c + 1) * HALF)
                    dve.tensor_tensor(yb_lo[:, cc], ybf[:], yb_hi[:, cc].bitcast(F32), ALU.subtract).then_inc(sem["yb_lo"], 1)

                def out_unit(w):
                    s = w % 2
                    per = 4 if s else 3
                    n = (w - 7) // 2
                    dve.wait_ge(out_stored[s], it * (16 * per) + 16 * (n + 1))
                    if w < 10:
                        leave(w, outr[:, s], wide(0))
                    else:
                        leave(w, outr[:, s, 0:M], ps[:, s, 0:M], Rm)

                neg_abs(0)
                softplus(0)
                softplus_lo(0)
                for s in range(SB_N):
                    if s + 1 < SB_N:
                        neg_abs(s + 1)
                    if s in (3, 6, 9):
                        out_unit(7 + s // 3 - 1)
                    if s == 10:
                        out_unit(10)
                        out_unit(11)
                    if s == 11:
                        out_unit(12)
                    log_a(s)
                    if s + 1 < SB_N:
                        softplus(s + 1)
                    a_lo(s)
                    if s == 4:
                        leave_o(3, 0)
                    if s + 1 < SB_N:
                        softplus_lo(s + 1)
                out_unit(13)
                leave_o(SB_N - 1, 1)
            assert seq["n"] == LINKS, seq["n"]
            seq["base"], seq["n"] = seq0 + HEADS * LINKS, 0

            for w in range(4):
                s = w % 2
                u = U_TAIL + w
                dve.wait_ge(sem["unit_done"], u + 1)
                scaled(tail[w][:], wide(2 * s), R[:]).then_inc(sem["pair_free"], 1)

            dve.wait_ge(sem["tail_stored"], 64)
            with dve.Fori(0, KT // 2) as p:
                for s in range(2):
                    n = p * 2 + s
                    dve.wait_ge(sem["unit_done"], n + (U_C + 1))
                    dve.wait_ge(sem["gates_sig"], n * 2 + 2)
                    dve.tensor_tensor(t1[s][:], wide(4 * s), ga[s][:], ALU.mult).then_inc(sem["t1_done"], 1)
                    dve.tensor_tensor(t2[s][:], wide(4 * s + 2), gb[s][:], ALU.mult).then_inc(sem["pair_free"], 1)
                    dve.wait_ge(sem["t1_done"], n + 1)
                    dve.wait_ge(sem["pair_free"], n + (U_C + 3))
                    dve.tensor_tensor(t1[s][:], t1[s][:], t2[s][:], ALU.add).then_inc(sem["m_done"], 1)
                    dve.wait_ge(sem["c_hi"], n + 1)
                    dve.tensor_tensor(A_lo[:, bass.ds(n, 1), :].rearrange("p o n -> p (o n)"), t1[s][:],
                                      A_hi[:, bass.ds(n, 1), :].rearrange("p o n -> p (o n)").bitcast(F32),
                                      ALU.subtract).then_inc(sem["c_lo"], 1)

            def one(t, n):
                return t[:, bass.ds(n, 1), :].rearrange("p o n -> p (o n)")

            def residual(u0, k, g, olds, where):
                dve.wait_ge(sem["norm_pe"], k) if k else None
                dve.memset(SQ[:], 0.0).then_inc(sem["sqz"], 1)
                dve.wait_ge(sem["sqz"], k + 1)
                with dve.Fori(0, KT // 2) as p:
                    for s in range(2):
                        n = p * 2 + s
                        i = n + k * KT
                        dve.wait_ge(sem["unit_done"], n + (u0 + 1))
                        dve.wait_ge(olds[s], p * 16 + (16 + k * (KT // 2) * 16))
                        if k == 0:
                            dve.wait_ge(new_stored[s], p * 16 + 16)
                        dve.tensor_tensor(where(n, s), wide(2 * s), old[s][:], ALU.add).then_inc(sem["pair_free"], 1)
                        dve.wait_ge(sem["g_hi"], i + 1)
                        dve.scalar_tensor_tensor(one(B_lo, n), where(n, s), vec[:, bass.ds(n + g, 1)],
                                                 one(B_hi, n).bitcast(F32), ALU.mult, ALU.subtract).then_inc(sem["g_lo"], 1)
                        dve.wait_ge(sem["sq_done"], i + 1)
                        dve.tensor_tensor(SQ[:], SQ[:], sq[:], ALU.add).then_inc(sem["sq_acc"], 1)
                        dve.wait_ge(sem["sq_acc"], i + 2)

            def rms(k):
                dve.wait_ge(sem["norm_sqrt"], 2 + k)
                dve.reciprocal(R[:], sq[:]).then_inc(sem["r_ready"], 1)
                dve.wait_ge(sem["r_ready"], k)

            olds = old_in
            residual(U_D, 0, V_XATTN, olds, lambda n, s: new[s][:])
            rms(1)
            dve.sem_inc(sem["oE_lo"], 1)
            with dve.Fori(0, HEADS) as h:
                for s in range(2):
                    dve.wait_ge(sem["unit_done"], h * 2 + (U_E + 1 + s))
                    if s == 0:
                        for t in new_stored:
                            dve.wait_ge(t, (KT // 2 + 1) * 16)
                    dve.scalar_tensor_tensor(qx[:, s], wide(2 * s), 1.0 / 16, R[:], ALU.mult, ALU.mult).then_inc(sem["pair_free"], 1)
                for hf in range(2):
                    i = h * 2 + hf
                    dve.wait_ge(sem["s_ready"], i + 1)
                    s4 = ps[:, 4:6, :].rearrange("p a (t m) -> p (a t) m", m=M)
                    dve.tensor_reduce(stat[:, 0, :], s4, AX_X, ALU.max).then_inc(sem["mx_done"], 1)
                    dve.wait_ge(sem["mx_done"], i + 1)
                    dve.tensor_scalar(stat[:, 1, :], stat[:, 0, :], -1.0, None, ALU.mult).then_inc(sem["nmx_done"], 1)
                    dve.wait_ge(sem["p_exp"], i + 1)
                    dve.reciprocal(stat[:, 3, :], stat[:, 2, :]).then_inc(sem["p_rec"], 1)
                    dve.wait_ge(sem["p_rec"], i + 1)
                    dve.tensor_tensor(px[:], px[:], stat[:, 3, :].unsqueeze(2).broadcast_to([P, 4, M]), ALU.mult)\
                       .then_inc(sem["p_done"], 1)
                    dve.wait_ge(sem["pT_pe"], i + 1)
                    dve.tensor_copy(pxT[:], ps[:, 6:8, :]).then_inc(sem["pT_done"], 1)
                    dve.wait_ge(sem["oE_hi"], i + 1)
                    dst = (slice(None), bass.ds(h * 2, 2), slice(hf * HALF, (hf + 1) * HALF))
                    dve.tensor_tensor(A_lo[dst], ps[:, 4:6, :], A_hi[dst].bitcast(F32), ALU.subtract).then_inc(sem["oE_lo"], 1)
            residual(U_F, 1, V_FFN, olds, lambda n, s: one(X, n))
            rms(2)
            u0 = U_G
            for gi, (f0, nf) in enumerate(GROUPS):
                with dve.Fori(0, nf) as f:
                    i = f + f0
                    dve.wait_ge(sem["unit_done"], f * 2 + (u0 + 1))
                    scaled(gt[:], wide(0), R[:]).then_inc(sem["pair_free"], 1)
                    dve.wait_ge(sem["unit_done"], f * 2 + (u0 + 2))
                    dve.wait_ge(sem["f_lo"], i + 1)
                    scaled(ut[:], wide(2), R[:]).then_inc(sem["pair_free"], 1)
                    dve.wait_ge(sem["f_silu"], i + 1)
                    dve.wait_ge(sem["pair_free"], f * 2 + (u0 + 4))
                    dve.tensor_tensor(ut[:], gt[:], ut[:], ALU.mult).then_inc(sem["f_prod"], 1)
                    dve.wait_ge(sem["f_hi"], i + 1)
                    dve.tensor_tensor(one(A_lo, f), ut[:], one(A_hi, f).bitcast(F32), ALU.subtract).then_inc(sem["f_lo"], 1)
                u1 = u0 + 2 * nf
                last = gi == len(GROUPS) - 1
                if last:
                    dve.memset(SQ[:], 0.0).then_inc(sem["sqz"], 1)
                    dve.wait_ge(sem["sqz"], 3)
                with dve.Fori(0, KT // 2) as p:
                    for s in range(2):
                        n = p * 2 + s
                        dve.wait_ge(sem["unit_done"], n + (u1 + 1))
                        dve.tensor_tensor(one(X, n), one(X, n), wide(2 * s), ALU.add).then_inc(sem["pair_free"], 1)
                        if last:
                            dve.wait_ge(sem["sq_done"], n + (2 * KT + 1))
                            dve.tensor_tensor(SQ[:], SQ[:], sq[:], ALU.add).then_inc(sem["sq_acc"], 1)
                            dve.wait_ge(sem["sq_acc"], n + (2 * KT + 2))
                u0 = u1 + KT
            rms(3)
            for n in range(KT):
                dve.scalar_tensor_tensor(X[:, n], X[:, n], vec[:, V_FINAL + n:V_FINAL + n + 1], R[:], ALU.mult, ALU.mult)\
                   .then_inc(sem["final_done"], 1)

        @block.scalar
        def _(act):
            def f(dst, src, func=ACT.Copy, **kw):
                return act.activation(dst, src, func, **kw)

            def waits_over():
                act.nop(nofuse=True)

            def one(t, n):
                return t[:, bass.ds(n, 1), :].rearrange("p o n -> p (o n)")

            def eps():
                return vec[:, V_EPS:V_EPS + 1]

            for t in out_stored + new_stored:
                act.sem_inc(t, 16)
            for n in ("y_stored", "yb_stored"):
                act.sem_inc(sem[n], 32)
            act.sem_inc(sem["z_copied"], 1)
            for c0, w, dst in ((C_MASK, (LEVELS + 1) * P, mask[:].rearrange("p a b -> p (a b)")), (C_RESET, T, reset[:]),
                               (C_SMASK, P, smask[:]), (C_NEGM, P, negm[:]), (C_ONES, P, ones[:]), (C_IDENT, P, ident[:]),
                               (C_NEGTRI, 2 * P, tri0[:].rearrange("p a b -> p (a b)"))):
                act.dma_start(dst, cst[:, c0:c0 + w]).then_inc(sem["cst_in"], 16)
            act.wait_ge(sem["vec_in"], 16)
            act.wait_ge(sem["lb_diff"], 1)
            f(lb[:, 1], lb[:, 1], ACT.Exp).then_inc(sem["lb_exp"], 1)
            f(lb[:, 2], lb[:, 2], ACT.Exp).then_inc(sem["lb_exp"], 1)

            def split_norm(src, g, hi, tmp, used):
                for k in range(KT):
                    f(hi[:, k], src[:, k], ACT.Copy, scale=vec[:, g + k:g + k + 1]).then_inc(sem["prep_act"], 1)
                    if k:
                        act.wait_ge(used, k)
                    f(tmp[:], src[:, k], ACT.Square).then_inc(sem["prep_act"], 1)

            act.wait_ge(sem["mem_in"], 16)
            split_norm(mem0, V_MEM, M_hi, sqm, sem["sqm_used"])
            act.wait_ge(sem["prep_pe"], 1)
            f(sqm[:], ps[:, 4, 0:M], ACT.Sqrt, scale=1.0 / D, bias=eps()).then_inc(sem["norm_sqrt"], 1)
            act.wait_ge(sem["x_in"], 16)
            split_norm(x0, V_MIX, A_hi, sq0, sem["sq0_used"])
            act.wait_ge(sem["prep_pe"], 2)
            f(sq0[:], wide(4), ACT.Sqrt, scale=1.0 / D, bias=eps()).then_inc(sem["norm_sqrt"], 1)
            act.wait_ge(sem["cst_in"], 7 * 16)
            f(negtri[:], tri0[:, 0])
            f(negrest[:], tri0[:, 1]).then_inc(sem["consts_cast"], 1)

            with act.Fori(0, HEADS) as it:
                U = it * PER_IT

                def left(i):
                    act.wait_ge(sem["pair_free"], U + (i + 3))

                left(0)
                act.wait_ge(sem["y_stored"], it * 32 + 32)
                f(El[0][:], fq[:], ACT.Exp, scale=-1.0).then_inc(sem["hgrn_exp"], 1)
                left(1)
                f(El[1][:], qh[:], ACT.Exp, scale=-1.0).then_inc(sem["hgrn_exp"], 1)
                left(3)
                f(QK[0][:], og[:], ACT.Exp, scale=-1.0).then_inc(sem["hgrn_exp"], 1)
                act.wait_ge(sem["hgrn_f"], it + 1)
                f(QK[1][:], bb[:], ACT.Ln).then_inc(sem["hgrn_lf"], 1)
                act.wait_ge(sem["iT_done"], it + 1)
                f(vtok[:].rearrange("p c v -> p (c v)"), wide(4)).then_inc(sem["vtok_copied"], 1)
                for lev in range(LEVELS):
                    m = CH >> (lev + 1)
                    act.wait_ge(sem["d_ready"], it * (LEVELS + 1) + lev + 1)
                    if lev >= 2:
                        act.wait_ge(sem["qk_ready"], it * LEVELS + lev - 1)
                    d, e = (x[:].rearrange("p (n h m) -> p n h m", h=2, m=m) for x in (Dl[lev % 2], El[lev % 2]))
                    f(e[:, :, 0], d[:, :, 0], ACT.Exp, scale=-1.0)
                    f(e[:, :, 1], d[:, :, 1], ACT.Exp).then_inc(sem["e_ready"], 1)
                act.wait_ge(sem["qk_ready"], it * LEVELS + LEVELS - 1)
                f(El[1][:], bb[:], ACT.Exp).then_inc(sem["e_ready"], 1)
                act.wait_ge(sem["d_ready"], it * (LEVELS + 1) + LEVELS + 1)
                act.wait_ge(sem["qk_ready"], it * LEVELS + LEVELS)
                f(El[0][:], Dl[0][:], ACT.Exp).then_inc(sem["e_ready"], 1)
                act.wait_ge(sem["keT_done"], it + 1)
                f(Ketok[:].rearrange("p c v -> p (c v)"), wide(6)).then_inc(sem["keT_copied"], 1)
                act.wait_ge(sem["o_done"], it + 1)
                f(QK[0][:], wide(6))
                f(QK[1][:], wide(6), ACT.Square).then_inc(sem["osq_ready"], 1)
                act.wait_ge(sem["hms_done"], it + 1)
                f(fq[:], wide(4), ACT.Ln, scale=1.0 / P, bias=eps()).then_inc(sem["hln"], 1)
                act.wait_ge(sem["hln"], it + 1)
                f(fq[:], fq[:], ACT.Exp, scale=-0.5).then_inc(sem["hr_ready"], 1)
                act.wait_ge(sem["y_f32"], it + 1)
                f(ya_hi[:], QK[0][:]).then_inc(sem["y_hi_done"], 1)
                act.wait_ge(sem["y_lo_done"], it + 1)
                act.dma_start(row(y_d[0], it), ya_hi[:].bitcast(F32)).then_inc(sem["y_stored"], 16)
                act.dma_start(row(y_d[1], it), ya_lo[:].bitcast(F32)).then_inc(sem["y_stored"], 16)

                h0, h1 = slice(0, 64), slice(64, 128)
                for dst, src in ((K2[h0, 0], kf[h0]), (K2[h1, 1], kf[h1]), (Q2h[h0, 0], qf[h0]), (Q2h[h1, 0], qf[h0]),
                                 (Q2h[h1, 1], qf[h1]), (Q2h[h0, 1], qf[h1])):
                    f(dst, src).then_inc(sem["kq_hi"], 1)
                act.wait_ge(sem["vT_done"], it + 1)
                vps = ps[:, 4:6, :].rearrange("p a (c h d) -> p (a c) h d", h=2, d=64)
                f(V2[:, :, :, 0:64], vps).then_inc(sem["v_hi"], 1)

                def cols(s):
                    c, j = SB_STEPS[s]
                    return max(0, j * P - c * HALF)

                def front(s):
                    g = it * SB_N + s
                    if s >= 2:
                        act.wait_ge(sem["al_done"], g - 1)
                    act.wait_ge(sem["z_done"], g + 1)
                    f(zs[s % 2][:, :, cols(s):], ps[:, 2:4, cols(s):HALF]).then_inc(sem["z_copied"], 1)
                    act.wait_ge(sem["nu_done"], g + 1)
                    e = el[s % 2][:, :, cols(s):]
                    f(e, e, ACT.Exp).then_inc(sem["ex_done"], 1)
                    act.wait_ge(sem["ex_done"], g + 1)
                    f(e, e, ACT.Ln, bias=1.0).then_inc(sem["ln_done"], 1)

                def softplus_hi(s):
                    g = it * SB_N + s
                    act.wait_ge(sem["sp_done"], g + 1)
                    if s:
                        act.wait_ge(sem["cum1_done"], g)
                        act.wait_ge(sem["cum2_done"], it * (SB_N - 2) + sum(j > 0 for _, j in SB_STEPS[:s]))
                    f(sph[:, :, cols(s):], el[s % 2][:, :, cols(s):]).then_inc(sem["sph_done"], 1)

                def weights_hi(s):
                    g = it * SB_N + s
                    act.wait_ge(sem["la_done"], g + 1)
                    z = zs[s % 2][:, :, cols(s):]
                    f(z, z, ACT.Exp).then_inc(sem["a_done"], 1)
                    act.wait_ge(sem["a_done"], g + 1)
                    if s:
                        act.wait_ge(sem["av_done"], g)
                    else:
                        act.wait_ge(sem["y_stored"], it * 32 + 64)
                    f(ah[:, :, cols(s):], z).then_inc(sem["ah_done"], 1)

                def y_hi(c):
                    act.wait_ge(sem["yb_f32"], it * 4 + 2 * c + 2)
                    f(yb_hi[:, c * HALF:(c + 1) * HALF], ybf[:]).then_inc(sem["yb_hi"], 1)

                def store(w):
                    left(w)
                    s = w % 2
                    if w < 10:
                        act.dma_start(row(gate_d, it * 3 + (w - 7)), outr[:, s]).then_inc(out_stored[s], 16)
                    else:
                        to = it * 2 + (w - 10 if w < 12 else w - 12 + KT)
                        act.dma_start(row(kv_d, to), outr[:, s, 0:M]).then_inc(out_stored[s], 16)

                front(0)
                softplus_hi(0)
                for s in range(SB_N):
                    if s + 1 < SB_N:
                        front(s + 1)
                    weights_hi(s)
                    if s in (3, 6, 9):
                        store(7 + s // 3 - 1)
                    if s == 10:
                        store(10)
                        store(11)
                    if s == 11:
                        store(12)
                    if s == 4:
                        y_hi(0)
                    if s + 1 < SB_N:
                        softplus_hi(s + 1)
                store(13)
                y_hi(1)
                act.wait_ge(sem["yb_lo"], it * 2 + 2)
                act.dma_start(row(y_d[0], it + HEADS), yb_hi[:].bitcast(F32)).then_inc(sem["yb_stored"], 16)
                act.dma_start(row(y_d[1], it + HEADS), yb_lo[:].bitcast(F32)).then_inc(sem["yb_stored"], 16)

            act.wait_ge(sem["y_stored"], (HEADS + 1) * 32)
            act.wait_ge(sem["yb_stored"], (HEADS + 1) * 32)
            act.wait_ge(out_stored[0], 16 * (3 * HEADS + 1))
            act.wait_ge(out_stored[1], 16 * (4 * HEADS + 1))
            act.dma_start(B_hi[:].bitcast(F32), y_d[0].rearrange("k p t -> p k t")).then_inc(sem["y_loaded"], 16)
            act.dma_start(B_lo[:].bitcast(F32), y_d[1].rearrange("k p t -> p k t")).then_inc(sem["y_loaded"], 16)

            def load_gates(n, s):
                act.dma_start(ga[s][:], row(gate_d, n)).then_inc(ga_in[s], 16)
                act.dma_start(gb[s][:], row(gate_d, n + KT)).then_inc(gb_in[s], 16)

            for s in range(2):
                load_gates(s, s)
            for w in range(4):
                act.wait_ge(sem["pair_free"], U_TAIL + w + 3)
                act.dma_start(gate_d[12 + w], tail[w][:]).then_inc(sem["tail_stored"], 16)
            act.wait_ge(sem["tail_stored"], 64)

            def gate_tiles(p, more):
                for s in range(2):
                    n = p * 2 + s
                    act.wait_ge(ga_in[s], p * 16 + 16)
                    f(ga[s][:], ga[s][:], ACT.Sigmoid).then_inc(sem["gates_sig"], 1)
                    act.wait_ge(gb_in[s], p * 16 + 16)
                    f(gb[s][:], gb[s][:], ACT.Sigmoid).then_inc(sem["gates_sig"], 1)
                    act.wait_ge(sem["m_done"], n + 1)
                    waits_over()
                    f(one(A_hi, n), t1[s][:]).then_inc(sem["c_hi"], 1)
                    if more:
                        load_gates(n + 2, s)

            with act.Fori(0, KT // 2 - 1) as p:
                gate_tiles(p, True)
            gate_tiles(KT // 2 - 1, False)

            def residual(u0, k, g, src, where, store_new):
                for s in range(2):
                    act.dma_start(old[s][:], src(s)).then_inc(old_in[s], 16)

                def tiles(p, more):
                    for s in range(2):
                        n = p * 2 + s
                        act.wait_ge(sem["pair_free"], n + (u0 + 3))
                        if more:
                            act.dma_start(old[s][:], src(n + 2)).then_inc(old_in[s], 16)
                        if store_new:
                            act.dma_start(row(x1_d, n), where(n, s)).then_inc(new_stored[s], 16)
                        waits_over()
                        f(one(B_hi, n), where(n, s), ACT.Copy, scale=vec[:, bass.ds(n + g, 1)]).then_inc(sem["g_hi"], 1)
                        act.wait_ge(sem["sq_acc"], n + (k * KT + 1))
                        waits_over()
                        f(sq[:], where(n, s), ACT.Square).then_inc(sem["sq_done"], 1)

                with act.Fori(0, KT // 2 - 1) as p:
                    tiles(p, True)
                tiles(KT // 2 - 1, False)

            def rms(k):
                act.wait_ge(sem["norm_pe"], k)
                f(sq[:], wide(4), ACT.Sqrt, scale=1.0 / D, bias=eps()).then_inc(sem["norm_sqrt"], 1)

            residual(U_D, 0, V_XATTN, lambda n: one(xT, n), lambda n, s: new[s][:], True)
            rms(1)

            with act.Fori(0, HEADS) as h:
                act.wait_ge(sem["oE_lo"], h * 2 + 1)
                act.dma_start(kx[:], kv_d[bass.ds(h * 2, 2)].rearrange("k p m -> p k m")).then_inc(sem["kv_in"], 16)
                act.dma_start(vx[:], kv_d[bass.ds(h * 2 + KT, 2)].rearrange("k p m -> p k m")).then_inc(sem["kv_in"], 16)
                act.wait_ge(sem["vtokE_pe"], h + 1)
                f(vxt[:].rearrange("p a m -> p (a m)"), ps[:, 6, :]).then_inc(sem["vtokE_done"], 1)
                for hf in range(2):
                    i = h * 2 + hf
                    act.wait_ge(sem["nmx_done"], i + 1)
                    for tt in range(4):
                        ins = f(px[:, tt], ps[:, 4 + tt // 2, (tt % 2) * M:(tt % 2 + 1) * M], ACT.Exp,
                                bias=stat[:, 1, tt:tt + 1], accum_out=stat[:, 2, tt:tt + 1])
                    ins.then_inc(sem["p_exp"], 1)
                    act.wait_ge(sem["oE_pe"], i + 1)
                    waits_over()
                    f(A_hi[:, bass.ds(h * 2, 2), hf * HALF:(hf + 1) * HALF], ps[:, 4:6, :]).then_inc(sem["oE_hi"], 1)
            residual(U_F, 1, V_FFN, lambda n: row(x1_d, n), lambda n, s: one(X, n), False)
            rms(2)
            u0 = U_G
            for gi, (f0, nf) in enumerate(GROUPS):
                with act.Fori(0, nf) as ff:
                    act.wait_ge(sem["pair_free"], ff * 2 + (u0 + 3))
                    f(gt[:], gt[:], ACT.Silu).then_inc(sem["f_silu"], 1)
                    act.wait_ge(sem["f_prod"], ff + (f0 + 1))
                    waits_over()
                    f(one(A_hi, ff), ut[:]).then_inc(sem["f_hi"], 1)
                u1 = u0 + 2 * nf
                if gi == len(GROUPS) - 1:
                    with act.Fori(0, KT) as n:
                        act.wait_ge(sem["pair_free"], n + (u1 + 3))
                        act.wait_ge(sem["sq_acc"], n + (2 * KT + 1))
                        waits_over()
                        f(sq[:], one(X, n), ACT.Square).then_inc(sem["sq_done"], 1)
                u0 = u1 + KT
            rms(3)
            for n in range(KT):
                act.wait_ge(sem["final_done"], n + 1)
                act.dma_start(out[n], X[:, n]).then_inc(sem["stored"], 16)
            act.wait_ge(sem["stored"], KT * 16)


def _tiles(w, n):
    c = w[:, n * P:(n + 1) * P].reshape(-1, P, P).transpose(1, 0, 2)
    u = np.zeros((P, KT, P), np.float32)
    u[:, :c.shape[1]] = c
    return u.reshape(P, D)


def _stream(w_in, w_gate, w_proj_a, w_proj_b, w_out, w_xq, w_xkv, w_xo, w_ffn_in, w_ffn_out):
    units = []
    col = lambda part, h: part * HEADS + h
    for h in range(HEADS):
        units += [_tiles(w_in, col(part, h)) for part in (1, 0, 2, 3, 4, 5, 6)]
        units += [_tiles(w_gate, 3 * h + g) for g in range(3)]
        units += [_tiles(w_xkv, n) for n in (2 * h, 2 * h + 1, KT + 2 * h, KT + 2 * h + 1)]
    units += [_tiles(w_gate, 12 + g) for g in range(4)]
    for n in range(KT):
        units.append(_tiles(np.concatenate([w_proj_a, w_proj_b], 0), n))
    for w in (w_out, w_xq, w_xo):
        units += [_tiles(w, n) for n in range(KT)]
    for f0, nf in GROUPS:
        for f in range(f0, f0 + nf):
            units += [_tiles(w_ffn_in, f), _tiles(w_ffn_in, FT + f)]
        units += [_tiles(w_ffn_out[f0 * P:(f0 + nf) * P], n) for n in range(KT)]
    return np.stack(units)


def kernel(x, mem, g_mix, w_in, lb_table, g_hgrn, w_gate, w_proj_a, w_proj_b, w_out,
           g_xattn, g_mem, w_xq, w_xkv, w_xo, g_ffn, w_ffn_in, w_ffn_out, g_final):
    import concourse.bacc as bacc
    from concourse.bass_utils import run_bass_kernel_spmd

    def a(v):
        return np.ascontiguousarray(v)

    def feature_major(v):
        return np.ascontiguousarray(a(v)[0].T.reshape(KT, P, -1).transpose(1, 0, 2))

    def columns(v):
        return a(v).reshape(-1, P).T

    vecs = np.concatenate([columns(v) for v in (g_mix, g_xattn, g_mem, g_ffn, g_final, g_hgrn, a(lb_table)[0], a(lb_table)[1])]
                          + [np.full((P, V_ALL - V_EPS), EPS, np.float32)], 1)
    arrays = {
        "x_t": feature_major(x), "mem_t": feature_major(mem), "vectors": np.ascontiguousarray(vecs), "constants": constants(),
        "weights": _stream(*(a(w)[0] for w in (w_in, w_gate, w_proj_a, w_proj_b, w_out, w_xq, w_xkv, w_xo, w_ffn_in, w_ffn_out))),
    }
    nc = bacc.Bacc("TRN2", target_bir_lowering=False, num_devices=1)
    args = [nc.dram_tensor(n, v.shape, F32, kind="ExternalInput").ap() for n, v in arrays.items()]
    out = nc.dram_tensor("out_t", (KT, P, T), F32, kind="ExternalOutput").ap()
    build(nc, *args, out)
    r = run_bass_kernel_spmd(nc, [arrays], core_ids=[0])
    return np.ascontiguousarray(r.results[0]["out_t"].reshape(D, T).T)[None]
```

```python
from contextlib import ExitStack

import concourse.bass as bass
from concourse import mybir
import numpy as np

ALU = mybir.AluOpType
ACT = mybir.ActivationFunctionType
F32 = mybir.dt.float32
F32R = mybir.dt.float32r
I32 = mybir.dt.int32
AX_X = mybir.AxisListType.X

P = 128
D = 1024
T = 1024
KT = D // P
HALF = 512
M = 256
HEADS = 4
CH = 128
NCH = T // CH
LEVELS = 7
DFF = 2816
FT = DFF // P
GROUPS = [(0, 8), (8, 7), (15, 7)]
EPS = 1e-6
NEG = -1e30
TINY = 2.0 ** -64

PROLOGUE = 4
PER_IT = 10
U_KV = PROLOGUE + HEADS * PER_IT - 4
U_TAIL = U_KV + 2 * KT
U_C = U_TAIL + 4
U_D = U_C + KT
U_E = U_D + KT
U_F = U_E + KT
U_G = U_F + KT
UNITS = U_G + 2 * FT + len(GROUPS) * KT

C_MASK, C_RESET, C_NEGTRI, C_NEGREST, C_SMASK, C_NEGM, C_ONES, C_IDENT = 0, 1024, 2048, 2176, 2304, 2432, 2560, 2688
C_ALL = 2816
V_MIX, V_XATTN, V_MEM, V_FFN, V_FINAL, V_HGRN, V_LB0, V_LB1, V_EPS = 0, 8, 16, 24, 32, 40, 44, 48, 52
V_ALL = 56

SB_STEPS = [(0, j) for j in range(3, -1, -1)] + [(1, j) for j in range(7, -1, -1)]
SB_N = len(SB_STEPS)
SB_LATE = 3
SB_DIAGONAL = [j * P >= c * HALF for c, j in SB_STEPS]


def sb_columns(s):
    c, j = SB_STEPS[s]
    return max(0, j * P - c * HALF)


def sb_fill(i, last):
    if last:
        return max(0, i - SB_LATE) * 2 * KT * KT // (2 * SB_N + 1 - SB_LATE)
    return i * 4 * KT // (2 * SB_N + 1)


def kv_done(i):
    return sb_fill(i, True) // KT


def constants():
    c = np.zeros((P, C_ALL), np.float32)
    s, t = np.arange(P)[:, None], np.arange(P)[None, :]
    for lev in range(LEVELS):
        m = CH >> (lev + 1)
        pair = (s // (2 * m) == t // (2 * m)) & (s % (2 * m) < m) & (t % (2 * m) >= m)
        c[:, C_MASK + lev * P:C_MASK + (lev + 1) * P] = pair
    c[:, C_MASK + LEVELS * P:C_MASK + (LEVELS + 1) * P] = s == t
    c[:, C_RESET:C_RESET + T] = (np.arange(T) % CH != 0)[None, :]
    c[:, C_NEGTRI:C_NEGTRI + P] = -1.0 * (s >= t)
    c[:, C_NEGREST:C_NEGREST + P] = -1.0 * (s < t)
    c[:, C_SMASK:C_SMASK + P] = s < t
    c[:, C_NEGM:C_NEGM + P] = NEG * (s >= t)
    c[:, C_ONES:C_ONES + P] = 1.0
    c[:, C_IDENT:C_IDENT + P] = s == t
    return c


SEMS = """
cst_in vec_in mem_in x0_in x1_in x2_in x3_in raw0_in raw1_in
w_hi_made weights_ready unit_done pair_free dve_seq
lb_diff lb_exp consts_cast x_lo x_sq x_hi x_sq_made m_lo m_sq m_hi m_sq_made norm0_pe m_stored m_loaded h_ready
hgrn_sig hgrn_f hgrn_lf
iT_done vtok_copied at_zero d_ready e_ready qk_ready s_done pred_done
qe_ready ke_ready keT_done keT_copied u_done state_ready o_done osq_ready hms_done hln hr_ready
y_f32 y_hi_done y_lo_done y_stored
kq_hi kq_lo vT_done v_hi v_lo
z_done z_copied nu_done ex_done ln_done sp_pre sp_done sph_done spl_done cum1_done la_pre la_done cum2_done
a_done ah_done al_done av_done yb_f32 yb_hi yb_lo yb_stored
out0_stored out1_stored tail_stored y_loaded
ga0_in ga1_in gb0_in gb1_in gates_sig t1_done t2_done m_done c_hi c_lo kv0_stored kv1_stored kv2_stored kv3_stored
old0_in old1_in new0_stored new1_stored g_hi g_lo sq_done sq_acc sqz norm_pe norm_sqrt r_ready
kx_in vx_in vtokE_pe vtokE_done s_ready mx_done nmx_done p_exp p_rec p_done pT_pe pT_done oE_pe oE_hi oE_lo
f_silu f_prod f_hi f_lo final_done stored
""".split()


def build(nc, xT, memT, vecs, cst, weights, out):
    ctx = ExitStack()
    with ctx:
        sem = {n: ctx.enter_context(nc.semaphore(n)) for n in SEMS}

        base = (nc.sbuf_base + 31) // 32 * 32
        K = 1024

        def at(name, offset, shape, dt=F32):
            return nc.alloc_sbuf_tensor_at(name, shape, dt, offset=base + int(offset))

        A0, W0 = 0, 64 * K
        X0, T0 = W0 + 64 * K, W0 + 96 * K
        RING, R0, S0 = W0 + 112 * K, W0 + 136 * K, W0 + 140 * K
        A_hi, A_lo = at("A_hi", A0, [P, KT, T], F32R), at("A_lo", A0 + 32 * K, [P, KT, T], F32R)
        B_hi, B_lo = at("B_hi", W0, [P, KT, T], F32R), at("B_lo", W0 + 32 * K, [P, KT, T], F32R)
        X = at("X", X0, [P, KT, T])
        raw = at("raw", RING, [P, 2, D])
        w_hi = at("w_hi", RING + 8 * K, [P, 2, D], F32R)
        w_lo = at("w_lo", RING + 16 * K, [P, 2, D], F32R)
        R = at("R", R0, [P, T])
        vec = at("vec", S0, [P, V_ALL])
        lb = at("lb", S0 + 256, [P, 4, 4])
        ones = at("ones", S0 + 512, [P, P])
        ident = at("ident", S0 + 1024, [P, P])
        stat = at("stat", S0 + 1536, [P, 4, 4])

        P0, U0 = W0 + 28 * K, W0 + 44 * K
        mask = at("mask", W0, [P, LEVELS + 1, P])
        reset = at("reset", W0 + 4 * K, [P, T])
        outr = at("outr", W0 + 8 * K, [P, 2, T])
        negtri = at("negtri", W0 + 16 * K, [P, P], F32R)
        negrest = at("negrest", W0 + 16 * K + 512, [P, P], F32R)
        smask = at("smask", W0 + 17 * K, [P, P])
        negm = at("negm", W0 + 17 * K + 512, [P, P])
        qf, kf = at("qf", W0 + 18 * K, [P, T]), at("kf", W0 + 22 * K, [P, T])
        yb_hi, yb_lo = at("yb_hi", W0 + 18 * K, [P, T], F32R), at("yb_lo", W0 + 22 * K, [P, T], F32R)
        ybf = at("ybf", W0 + 26 * K, [P, HALF])
        fq, iv, qh, og = (at(n, P0 + 4 * i * K, [P, T]) for i, n in enumerate(("fq", "iv", "qh", "og")))
        Dl = [fq, iv]
        kk, bb = at("kk", U0, [P, T]), at("bb", U0 + 4 * K, [P, T])
        vtok, AT = at("vtok", U0 + 8 * K, [P, NCH, P]), at("AT", U0 + 12 * K, [P, NCH, P])
        Qe, Ke = at("Qe", U0 + 16 * K, [P, T]), at("Ke", U0 + 20 * K, [P, T])
        Ketok, St = at("Ketok", U0 + 24 * K, [P, NCH, P]), at("St", U0 + 28 * K, [P, NCH, P])
        vf = at("vf", U0 + 32 * K, [P, T])
        QK = [at(f"QK{i}", U0 + (36 + 4 * i) * K, [P, T]) for i in range(2)]
        El = [at(f"El{i}", U0 + (44 + 4 * i) * K, [P, T]) for i in range(2)]
        of, rf = at("of", U0 + 52 * K, [P, T]), at("rf", U0 + 56 * K, [P, T])
        ya_hi, ya_lo = at("ya_hi", U0 + 60 * K, [P, T], F32R), at("ya_lo", U0 + 64 * K, [P, T], F32R)
        K2 = at("K2", U0, [P, 2, T], F32R)
        Q2h, Q2l = at("Q2h", U0 + 8 * K, [P, 2, T], F32R), at("Q2l", U0 + 16 * K, [P, 2, T], F32R)
        V2 = at("V2", U0 + 24 * K, [P, NCH, 2, P], F32R)
        zs = [at(f"zs{i}", U0 + (32 + 4 * i) * K, [P, 2, HALF]) for i in range(3)]
        el = [at(f"el{i}", U0 + (44 + 4 * i) * K, [P, 2, HALF]) for i in range(3)]
        spl = [at(f"spl{i}", U0 + (44 + 4 * i) * K, [P, 2, HALF], F32R) for i in range(3)]
        sph = [at(f"sph{i}", U0 + (56 + 4 * i) * K, [P, 2, HALF], F32R) for i in range(2)]
        ah = at("ah", U0 + 64 * K, [P, 2, HALF], F32R)
        al = at("al", W0 + 8 * K, [P, 2, HALF], F32R)
        M_hi, M_lo = at("M_hi", P0, [P, KT, M], F32R), at("M_lo", P0 + 8 * K, [P, KT, M], F32R)
        kvo = at("kvo", W0 + 4 * K, [P, 4, M])
        x0 = at("x0", U0, [P, KT, T])
        sq0, SQ0 = at("sq0", U0 + 32 * K, [P, T]), at("SQ0", U0 + 36 * K, [P, T])
        mem0 = at("mem0", U0 + 40 * K, [P, KT, M])
        M0_hi, M0_lo = at("M0_hi", U0 + 48 * K, [P, KT, M], F32R), at("M0_lo", U0 + 56 * K, [P, KT, M], F32R)
        sqm, SQm = at("sqm", U0 + 64 * K, [P, M]), at("SQm", U0 + 65 * K, [P, M])
        tri0 = at("tri0", U0 + 66 * K, [P, 2, P])
        Rm = at("Rm", S0 + 1536 + 256, [P, M])
        ga = [at(f"ga{i}", X0 + 4 * i * K, [P, T]) for i in range(2)]
        gb = [at(f"gb{i}", X0 + (8 + 4 * i) * K, [P, T]) for i in range(2)]
        t1 = [at(f"t1{i}", X0 + (16 + 4 * i) * K, [P, T]) for i in range(2)]
        t2 = at("t2", X0 + 24 * K, [P, T])
        tail = at("tail", T0, [P, 4, T])
        old = [at(f"old{i}", T0 + 4 * i * K, [P, T]) for i in range(2)]
        sq, SQ = at("sq", T0 + 8 * K, [P, T]), at("SQ", T0 + 12 * K, [P, T])
        new = [at(f"new{i}", X0 + 4 * i * K, [P, T]) for i in range(2)]
        qx = at("qx", X0, [P, 2, T])
        kx = at("kx", X0 + 8 * K, [P, KT, M])
        vx = at("vx", X0 + 16 * K, [P, 2, M])
        vxt = at("vxt", X0 + 18 * K, [P, 2, M])
        px = at("px", X0 + 20 * K, [P, 4, M])
        pxT = at("pxT", X0 + 24 * K, [P, 2, HALF])
        gt, ut = at("gt", T0, [P, T]), at("ut", T0 + 4 * K, [P, T])

        ps = ctx.enter_context(nc.psum_tensor("ps", [P, 8, HALF], F32))

        def wide(b):
            return ps[:, b:b + 2, :].rearrange("p a b -> p (a b)")

        gate_d = nc.dram_tensor("gate_d", [16, P, T], F32).ap()
        kv_d = nc.dram_tensor("kv_d", [16, P, M], F32).ap()
        y_d = nc.dram_tensor("y_d", [2, 8, P, T], F32).ap()
        m_d = nc.dram_tensor("m_d", [2, P, KT, M], F32).ap()
        x1_d = nc.dram_tensor("x1_d", [KT, P, T], F32).ap()

        def row(t, i):
            return t[bass.ds(i, 1)].rearrange("o p n -> p (o n)")

        block = ctx.enter_context(nc.Block())
        raw_in = [sem["raw0_in"], sem["raw1_in"]]
        out_stored = [sem["out0_stored"], sem["out1_stored"]]
        new_stored = [sem["new0_stored"], sem["new1_stored"]]
        x_in = [sem[f"x{i}_in"] for i in range(4)]
        kv_stored = [sem[f"kv{i}_stored"] for i in range(4)]
        old_in = [sem["old0_in"], sem["old1_in"]]
        ga_in, gb_in = [sem["ga0_in"], sem["ga1_in"]], [sem["gb0_in"], sem["gb1_in"]]

        @block.sync
        def _(sp):
            sp.dma_start(vec[:], vecs).then_inc(sem["vec_in"], 16)
            sp.dma_start(raw[:, 0], weights[0]).then_inc(raw_in[0], 16)
            for i in range(4):
                sp.dma_start(x0[:, 2 * i:2 * i + 2], xT[:, 2 * i:2 * i + 2]).then_inc(x_in[i], 16)
                if i == 0:
                    sp.dma_start(raw[:, 1], weights[1]).then_inc(raw_in[1], 16)
            sp.dma_start(mem0[:], memT).then_inc(sem["mem_in"], 16)
            with sp.Fori(1, UNITS // 2) as p:
                for s in range(2):
                    sp.wait_ge(sem["weights_ready"], p * 2 + (s - 1))
                    sp.dma_start(raw[:, s], row(weights, p * 2 + s)).then_inc(raw_in[s], 16)

        @block.gpsimd
        def _(pool):
            def split(u, s, n, first):
                pool.wait_ge(raw_in[s], n * 16 + 16)
                if not first:
                    pool.wait_ge(sem["unit_done"], u - 1)
                pool.nop(nofuse=True)
                pool.tensor_copy(w_hi[:, s], raw[:, s]).then_inc(sem["w_hi_made"], 1)
                pool.wait_ge(sem["w_hi_made"], u + 1)
                pool.tensor_tensor(w_lo[:, s], raw[:, s], w_hi[:, s].bitcast(F32),
                                   ALU.subtract).then_inc(sem["weights_ready"], 1)

            for s in range(2):
                split(s, s, 0, True)
            with pool.Fori(1, UNITS // 2) as p:
                for s in range(2):
                    split(p * 2 + s, s, p, False)

        @block.tensor
        def _(pe):
            def k_steps(u, s, hi, lo, dest, k0, k1, kts=KT, kb=0, last=True, ready=None):
                for k in range(k0, k1):
                    if ready:
                        pe.wait_ge(sem[ready[0]], ready[1] + k)
                    wh, wl = (w[:, s, (kb + k) * P:(kb + k + 1) * P] for w in (w_hi, w_lo))
                    for n, (w, a) in enumerate(((wh, hi), (wh, lo), (wl, hi))):
                        for c, (bank, cols) in enumerate(dest):
                            mm = pe.matmul(bank, w, a[:, k, cols], start=(k == 0 and n == 0),
                                           stop=(k == kts - 1 and n == 2), skip_group_check=True)
                if k1 == kts and last:
                    mm.then_inc(sem["unit_done"], 1)

            def halves(b):
                return [(ps[:, b, :], slice(0, HALF)), (ps[:, b + 1, :], slice(HALF, T))]

            def begin(u, since=2):
                pe.wait_ge(sem["weights_ready"], u + 1)
                pe.wait_ge(sem["pair_free"], u + (3 - since))

            def unit(u, s, hi, lo, b, since=2, kts=KT, ready=None):
                begin(u, since)
                k_steps(u, s, hi, lo, halves(b), 0, kts, kts=kts, ready=ready)

            def norm_sum(acc, cols, b):
                n = min(cols, HALF)
                for c in range(cols // n):
                    mm = pe.matmul(ps[:, b + c, 0:n], ones[:], acc[:, c * n:(c + 1) * n], start=True, stop=True)
                return mm

            for w in range(PROLOGUE):
                unit(w, w % 2, A_hi, A_lo, 2 * (w % 2), ready=("x_lo", 1))
                if w == 0:
                    pe.wait_ge(sem["cst_in"], 7 * 16)
                    pe.wait_ge(sem["x_sq"], KT)
                    norm_sum(SQ0, T, 4).then_inc(sem["norm0_pe"], 1)
                if w == PROLOGUE - 1:
                    pe.wait_ge(sem["m_sq"], KT)
                    norm_sum(SQm, M, 6).then_inc(sem["norm0_pe"], 1)
            pe.wait_ge(sem["consts_cast"], 1)
            pe.wait_ge(sem["norm_sqrt"], 2)

            def head_round(it, last):
                U = it * PER_IT + PROLOGUE
                pe.wait_ge(sem["pair_free"], U + 1)
                pe.wait_ge(sem["yb_f32"], it * 4 + 4)
                for c in range(NCH):
                    mm = pe.transpose(ps[:, 4 + c // 4, (c % 4) * P:(c % 4 + 1) * P], iv[:, c * P:(c + 1) * P], ident[:])
                mm.then_inc(sem["iT_done"], 1)

                def fill(first, k0, k1, since=2):
                    for n in range(k0, k1):
                        w, k = first + n // KT, n % KT
                        if k == 0:
                            begin(U + w, since)
                        k_steps(U + w, w % 2, A_hi, A_lo, halves(2 * (w % 2)), k, k + 1)

                pe.wait_ge(sem["z_copied"], it * SB_N + 1)
                fill(0, 0, KT)
                for lev in range(LEVELS + 1):
                    b = 4 + 2 * ((lev + 1) % 2)
                    if lev < LEVELS:
                        pe.wait_ge(sem["qk_ready"], it * LEVELS + lev + 1)
                        ks = qs = QK[lev % 2]
                    else:
                        ks, qs = kk, qh
                    if lev == 1:
                        pe.wait_ge(sem["vtok_copied"], it + 1)
                    elif lev >= 2:
                        pe.wait_ge(sem["pred_done"], it * (LEVELS + 1) + lev - 1)
                    for c in range(NCH):
                        mm = pe.matmul(ps[:, b + c // 4, (c % 4) * P:(c % 4 + 1) * P],
                                       ks[:, c * P:(c + 1) * P], qs[:, c * P:(c + 1) * P], start=True, stop=True)
                    mm.then_inc(sem["s_done"], 1)
                    fill(1, 2 * lev, 2 * lev + 2)

                pe.wait_ge(sem["ke_ready"], it + 1)
                pe.wait_ge(sem["pred_done"], it * (LEVELS + 1) + LEVELS)
                for c in range(NCH):
                    mm = pe.transpose(ps[:, 6 + c // 4, (c % 4) * P:(c % 4 + 1) * P], Ke[:, c * P:(c + 1) * P], ident[:])
                mm.then_inc(sem["keT_done"], 1)
                fill(3, 0, 2)
                pe.wait_ge(sem["keT_copied"], it + 1)
                pe.wait_ge(sem["pred_done"], it * (LEVELS + 1) + LEVELS + 1)
                for c in range(NCH - 1):
                    mm = pe.matmul(ps[:, 4 + c // 4, (c % 4) * P:(c % 4 + 1) * P], Ketok[:, c, :], vtok[:, c, :],
                                   start=True, stop=True)
                mm.then_inc(sem["u_done"], 1)
                fill(3, 2, 4)
                for c in range(NCH):
                    o = ps[:, 6 + c // 4, (c % 4) * P:(c % 4 + 1) * P]
                    mm = pe.matmul(o, vtok[:, c, :], AT[:, c, :], start=True, stop=(c == 0))
                    if c:
                        pe.wait_ge(sem["state_ready"], it * (NCH - 1) + c)
                        mm = pe.matmul(o, St[:, c, :], Qe[:, c * P:(c + 1) * P], start=False, stop=True)
                mm.then_inc(sem["o_done"], 1)
                fill(3, 4, 8)
                pe.wait_ge(sem["osq_ready"], it + 1)
                norm_sum(QK[1], T, 4).then_inc(sem["hms_done"], 1)

                for c in range(NCH):
                    mm = pe.transpose(ps[:, 6 + c // 4, (c % 4) * P:(c % 4 + 1) * P], vf[:, c * P:(c + 1) * P], ident[:])
                mm.then_inc(sem["vT_done"], 1)
                fill(4, 0, 16)
                pe.wait_ge(sem["pair_free"], U + 8)
                pe.wait_ge(sem["kq_lo"], it + 1)
                pe.wait_ge(sem["hr_ready"], it + 1)

                def scores(s):
                    c, j = SB_STEPS[s]
                    g = it * SB_N + s
                    if s:
                        pe.wait_ge(sem["z_copied"], g + 1)
                    for a in range(2):
                        for n, q in enumerate((Q2h, Q2l)):
                            mm = pe.matmul(ps[:, 2 + a, sb_columns(s):HALF], K2[:, a, j * P:(j + 1) * P],
                                           q[:, a, c * HALF + sb_columns(s):(c + 1) * HALF], start=(n == 0), stop=(n == 1))
                    mm.then_inc(sem["z_done"], 1)

                def cumulate(s, sel, name, first):
                    for a in range(2):
                        for n, x in enumerate((sph[s % 2], spl[s % 3])):
                            mm = pe.matmul(ps[:, 4 + a, sb_columns(s):HALF], sel[:], x[:, a, sb_columns(s):HALF],
                                           start=(first and n == 0), stop=True, skip_group_check=True)
                    mm.then_inc(sem[name], 1)

                def values(s):
                    c, j = SB_STEPS[s]
                    pe.wait_ge(sem["al_done"], it * SB_N + s + 1)
                    if s == 4:
                        pe.wait_ge(sem["yb_f32"], it * 4 + 6)
                    for a in range(2):
                        for n, x in enumerate((ah, al)):
                            mm = pe.matmul(ps[:, 6 + a, sb_columns(s):HALF], V2[:, j, a, :], x[:, a, sb_columns(s):HALF],
                                           start=(s in (0, 4) and n == 0), stop=True, skip_group_check=True)
                    mm.then_inc(sem["av_done"], 1)

                def fill_next(i):
                    for n in range(sb_fill(i, last), sb_fill(i + 1, last)):
                        w, k = 6 + n // KT, n % KT
                        if n == 0 and last:
                            pe.wait_ge(sem["m_loaded"], 32)
                        if k == 0:
                            begin(U + w, since=2 if last else 1)
                        if last:
                            k_steps(U + w, w % 2, M_hi, M_lo, [(ps[:, w % 2, 0:M], slice(0, M))], k, k + 1)
                        else:
                            k_steps(U + w, w % 2, A_hi, A_lo, halves(0), k, k + 1)

                def cumulate_block(s):
                    pe.wait_ge(sem["spl_done"], it * SB_N + s + 1)
                    if s == 4:
                        pe.wait_ge(sem["la_done"], it * SB_N + s)
                    cumulate(s, negtri, "cum1_done", s in (0, 4))

                pe.wait_ge(sem["v_lo"], it + 1)
                scores(0)
                scores(1)
                fill_next(0)
                scores(2)
                cumulate_block(0)
                for s in range(SB_N):
                    if SB_STEPS[s][1]:
                        pe.wait_ge(sem["la_done"], it * SB_N + s + 1)
                        cumulate(s, negrest, "cum2_done", False)
                    if s + 3 < SB_N:
                        scores(s + 3)
                    fill_next(2 * s + 1)
                    if s + 1 < SB_N:
                        cumulate_block(s + 1)
                    fill_next(2 * s + 2)
                    values(s)

            with pe.Fori(0, HEADS - 1) as it:
                head_round(it, False)
            head_round(HEADS - 1, True)

            pe.wait_ge(sem["pair_free"], U_TAIL + 2)
            pe.wait_ge(sem["z_copied"], HEADS * SB_N + 1)
            for i in range(4):
                unit(U_TAIL + i, i % 2, A_hi, A_lo, 2 * (i % 2))
            pe.wait_ge(sem["yb_f32"], HEADS * 4 + 4)
            pe.wait_ge(sem["pair_free"], U_C + 2)
            pe.wait_ge(sem["y_loaded"], 32)
            with pe.Fori(0, KT // 2) as p:
                for s in range(2):
                    u = p * 2 + (U_C + s)
                    begin(u)
                    k_steps(u, s, B_hi, B_lo, halves(4 * s), 0, 4, kts=4, last=False)
                    k_steps(u, s, B_hi[:, 4:8, :], B_lo[:, 4:8, :], halves(4 * s + 2), 0, 4, kts=4, kb=4)

            def linear(u0, hi, lo, ready):
                with pe.Fori(0, KT // 2) as p:
                    for s in range(2):
                        unit(p * 2 + (u0 + s), s, hi, lo, 2 * s, ready=ready)

            def norm_of(n):
                pe.wait_ge(sem["sq_acc"], n * KT + 1)
                norm_sum(SQ, T, 4).then_inc(sem["norm_pe"], 1)

            linear(U_D, A_hi, A_lo, ("c_lo", 1))
            norm_of(1)
            for s in range(2):
                unit(U_E + s, s, B_hi, B_lo, 2 * s, ready=("g_lo", 1))
            pe.wait_ge(sem["norm_sqrt"], 3)

            def attend(h, more):
                def fill(k0, k1):
                    for n in range(k0, k1) if more else ():
                        w, k = n // KT, n % KT
                        if k == 0:
                            begin(h * 2 + (U_E + 2 + w))
                        k_steps(h * 2 + (U_E + 2 + w), w, B_hi, B_lo, halves(2 * w), k, k + 1)

                def scores(hf):
                    if hf == 0:
                        pe.wait_ge(sem["pair_free"], h * 2 + (U_E + 4))
                    pe.wait_ge(sem["p_exp"], h * 2 + (hf + 1))
                    for tt in range(4):
                        for ds in range(2):
                            t = hf * HALF + tt * P
                            mm = pe.matmul(ps[:, 4 + tt // 2, (tt % 2) * M:(tt % 2 + 1) * M], qx[:, ds, t:t + P],
                                           kx[:, bass.ds(h * 2 + ds, 1), :].rearrange("p o m -> p (o m)"),
                                           start=(ds == 0), stop=(ds == 1))
                    mm.then_inc(sem["s_ready"], 1)

                def turn(hf):
                    pe.wait_ge(sem["p_done"], h * 2 + (hf + 1))
                    pe.wait_ge(sem["oE_lo"], h * 2 + (hf + 1))
                    for tt in range(4):
                        for mt in range(2):
                            mm = pe.transpose(ps[:, 6 + mt, tt * P:(tt + 1) * P], px[:, tt, mt * P:(mt + 1) * P], ident[:])
                    mm.then_inc(sem["pT_pe"], 1)

                def values(hf):
                    pe.wait_ge(sem["pT_done"], h * 2 + (hf + 1))
                    for ds in range(2):
                        for mt in range(2):
                            mm = pe.matmul(ps[:, 6 + ds, :], vxt[:, mt, ds * P:(ds + 1) * P], pxT[:, mt, :],
                                           start=(mt == 0), stop=(mt == 1))
                    mm.then_inc(sem["oE_pe"], 1)

                pe.wait_ge(sem["vx_in"], h * 16 + 16)
                pe.wait_ge(sem["kx_in"], 16)
                pe.wait_ge(sem["oE_lo"], h * 2 + 1)
                for ds in range(2):
                    for mt in range(2):
                        mm = pe.transpose(ps[:, 6, mt * M + ds * P:mt * M + (ds + 1) * P],
                                          vx[:, ds, mt * P:(mt + 1) * P], ident[:])
                mm.then_inc(sem["vtokE_pe"], 1)
                scores(0)
                fill(0, 5)
                pe.wait_ge(sem["vtokE_done"], h + 1)
                turn(0)
                scores(1)
                fill(5, 6)
                values(0)
                fill(6, 11)
                turn(1)
                fill(11, 13)
                values(1)
                fill(13, 16)

            with pe.Fori(0, HEADS - 1) as h:
                attend(h, True)
            attend(HEADS - 1, False)
            pe.wait_ge(sem["oE_lo"], 2 * HEADS + 1)
            linear(U_F, A_hi, A_lo, None)
            norm_of(2)
            u0 = U_G
            for f0, nf in GROUPS:
                with pe.Fori(0, nf) as f:
                    for s in range(2):
                        unit(f * 2 + (u0 + s), s, B_hi, B_lo, 2 * s, ready=("g_lo", KT + 1) if f0 == 0 else None)
                with pe.Fori(0, KT // 2) as p:
                    for s in range(2):
                        unit(p * 2 + (u0 + 2 * nf + s), s, A_hi, A_lo, 2 * s, kts=nf, ready=("f_lo", f0 + 2))
                u0 += 2 * nf + KT
            norm_of(3)

        @block.vector
        def _(dve):
            seq = {"base": 0, "n": 0}

            def link(ins):
                seq["n"] += 1
                ins.then_inc(sem["dve_seq"], 1)
                dve.wait_ge(sem["dve_seq"], seq["base"] + seq["n"])

            def scaled(dst, src, r):
                return dve.tensor_tensor(dst, src, r, ALU.mult)

            for n, v in (("pair_free", 2), ("sq_acc", 1), ("f_lo", 1), ("yb_f32", 4), ("oE_lo", 1)):
                dve.sem_inc(sem[n], v)
            dve.wait_ge(sem["vec_in"], 16)
            l0, l1 = vec[:, V_LB0:V_LB0 + 4], vec[:, V_LB1:V_LB1 + 4]
            link(dve.tensor_tensor(lb[:, 0], l0, l1, ALU.max))
            link(dve.tensor_tensor(lb[:, 1], l0, lb[:, 0], ALU.subtract))
            dve.tensor_tensor(lb[:, 2], l1, lb[:, 0], ALU.subtract).then_inc(sem["lb_diff"], 1)
            dve.wait_ge(sem["lb_exp"], 2)
            link(dve.tensor_tensor(lb[:, 0], lb[:, 1], lb[:, 2], ALU.add))
            link(dve.reciprocal(lb[:, 3], lb[:, 0]))
            link(dve.tensor_tensor(lb[:, 0], lb[:, 1], lb[:, 3], ALU.mult))
            link(dve.tensor_tensor(lb[:, 1], lb[:, 2], lb[:, 3], ALU.mult))

            def split_norm(src, g, hi, lo, tmp, acc, n):
                for k in range(KT):
                    dve.wait_ge(sem[f"{n}_hi"], k + 1)
                    dve.scalar_tensor_tensor(lo[:, k], src[:, k], vec[:, g + k:g + k + 1], hi[:, k].bitcast(F32),
                                             ALU.mult, ALU.subtract).then_inc(sem[f"{n}_lo"], 1)
                    dve.wait_ge(sem[f"{n}_sq_made"], k + 1)
                    if k == 0:
                        op = dve.tensor_copy(acc[:], tmp[:])
                    else:
                        dve.wait_ge(sem[f"{n}_sq"], k)
                        op = dve.tensor_tensor(acc[:], acc[:], tmp[:], ALU.add)
                    op.then_inc(sem[f"{n}_sq"], 1)

            split_norm(x0, V_MIX, A_hi, A_lo, sq0, SQ0, "x")
            dve.wait_ge(sem["norm_sqrt"], 1)
            link(dve.reciprocal(R[:], sq0[:]))

            def leave(u, dst, b, r=R):
                dve.wait_ge(sem["unit_done"], u + 1)
                dve.tensor_tensor(dst, b, r[:], ALU.mult).then_inc(sem["pair_free"], 1)

            leave(0, fq[:], wide(0))
            leave(1, qh[:], wide(2))
            split_norm(mem0, V_MEM, M0_hi, M0_lo, sqm, SQm, "m")
            leave(2, iv[:], wide(0))
            leave(3, og[:], wide(2))
            dve.wait_ge(sem["norm_sqrt"], 2)
            link(dve.reciprocal(Rm[:], sqm[:]))
            dve.wait_ge(sem["m_stored"], 32)

            seq0 = seq["n"]
            LINKS = 5
            def head_round(it, last):
                seq["base"], seq["n"] = it * LINKS + seq0, 0
                U = it * PER_IT + PROLOGUE

                dve.wait_ge(sem["hgrn_sig"], it * 3 + 1)
                link(dve.tensor_scalar(fq[:], fq[:], lb[:, 1, bass.ds(it, 1)], lb[:, 0, bass.ds(it, 1)], ALU.mult, ALU.add))
                dve.tensor_scalar(bb[:], fq[:], TINY, None, ALU.max).then_inc(sem["hgrn_f"], 1)
                dve.tensor_scalar(kk[:], fq[:], -1.0, 1.0, ALU.mult, ALU.add)
                dve.wait_ge(sem["hgrn_sig"], it * 3 + 3)
                dve.tensor_tensor(qh[:], qh[:], El[1][:], ALU.mult)
                dve.tensor_tensor(og[:], og[:], QK[0][:], ALU.mult)
                dve.memset(AT[:], 0.0).then_inc(sem["at_zero"], 1)
                dve.wait_ge(sem["hgrn_lf"], it + 1)
                link(dve.tensor_tensor_scan(bb[:], reset[:], QK[1][:], 0.0, ALU.mult, ALU.add))

                def diff(lev):
                    m = CH >> (lev + 1)
                    b3 = bb[:].rearrange("p (n w) -> p n w", w=2 * m)
                    d3 = Dl[lev % 2][:].rearrange("p (n w) -> p n w", w=2 * m)
                    n = T // (2 * m)
                    if lev == 1:
                        dve.wait_ge(sem["iT_done"], it + 1)
                    dve.tensor_tensor(d3, b3, b3[:, :, m - 1:m].broadcast_to([P, n, 2 * m]), ALU.subtract)\
                       .then_inc(sem["d_ready"], 1)

                def weigh(lev):
                    m = CH >> (lev + 1)
                    dve.wait_ge(sem["e_ready"], it * 9 + lev + 1)
                    if lev >= 2:
                        dve.wait_ge(sem["s_done"], it * (LEVELS + 1) + lev - 1)
                    e, k, q, o = (x[:].rearrange("p (n h m) -> p n h m", h=2, m=m) for x in (El[lev % 2], kk, qh, QK[lev % 2]))
                    dve.tensor_tensor(o[:, :, 0], e[:, :, 0], k[:, :, 0], ALU.mult)
                    dve.tensor_tensor(o[:, :, 1], e[:, :, 1], q[:, :, 1], ALU.mult).then_inc(sem["qk_ready"], 1)

                def pick(lev):
                    b = 4 + 2 * ((lev + 1) % 2)
                    dve.wait_ge(sem["s_done"], it * (LEVELS + 1) + lev + 1)
                    if lev:
                        dve.wait_ge(sem["pred_done"], it * (LEVELS + 1) + lev)
                    else:
                        dve.wait_ge(sem["at_zero"], it + 1)
                    dve.nop(nofuse=True)
                    dve.copy_predicated(AT[:], mask[:, lev, :].bitcast(I32).unsqueeze(1).broadcast_to([P, NCH, P]),
                                        ps[:, b:b + 2, :].rearrange("p a (c t) -> p (a c) t", t=P)).then_inc(sem["pred_done"], 1)

                diff(0)
                diff(1)
                weigh(0)
                for lev in range(1, LEVELS):
                    if lev + 1 < LEVELS:
                        diff(lev + 1)
                    weigh(lev)
                    pick(lev - 1)
                    if lev == 2:
                        dve.wait_ge(sem["yb_stored"], it * 32 + 32)
                        dve.wait_ge(sem["unit_done"], U + 1)
                        dve.scalar_tensor_tensor(qf[:], wide(0), 0.125, R[:], ALU.mult, ALU.mult).then_inc(sem["pair_free"], 1)
                    if lev == 6:
                        leave(U + 1, kf[:], wide(2))
                def out_unit(w):
                    s = w % 2
                    dve.wait_ge(out_stored[s], it * (16 * (2 if s else 1)) + 16 * ((w - 3) // 2 + 1))
                    leave(U + w, outr[:, s], wide(2 * s))

                b3 = bb[:].rearrange("p (n w) -> p n w", w=CH)
                dve.tensor_tensor(Dl[0][:].rearrange("p (n w) -> p n w", w=CH), b3[:, :, CH - 1:CH].broadcast_to([P, NCH, CH]),
                                  b3, ALU.subtract).then_inc(sem["d_ready"], 1)
                dve.wait_ge(sem["e_ready"], it * 9 + 8)
                dve.tensor_tensor(Qe[:], qh[:], El[1][:], ALU.mult).then_inc(sem["qe_ready"], 1)
                dve.wait_ge(sem["e_ready"], it * 9 + 9)
                dve.tensor_tensor(Ke[:], kk[:], El[0][:], ALU.mult).then_inc(sem["ke_ready"], 1)
                pick(LEVELS - 1)
                pick(LEVELS)
                leave(U + 2, vf[:], wide(0))
                dve.wait_ge(sem["u_done"], it + 1)
                for c in range(1, NCH):
                    u = ps[:, 4 + (c - 1) // 4, ((c - 1) % 4) * P:((c - 1) % 4 + 1) * P]
                    if c == 1:
                        dve.tensor_copy(St[:, 1, :], u).then_inc(sem["state_ready"], 1)
                    else:
                        dve.wait_ge(sem["state_ready"], it * (NCH - 1) + c - 1)
                        dve.scalar_tensor_tensor(St[:, c, :], St[:, c - 1, :], El[1][:, c * P - 1:c * P], u,
                                                 ALU.mult, ALU.add).then_inc(sem["state_ready"], 1)
                out_unit(3)

                dve.wait_ge(sem["kq_hi"], it * 6 + 6)
                lo_of = lambda dst, src, hi: dve.tensor_tensor(dst, src, hi.bitcast(F32), ALU.subtract)
                h0, h1 = slice(0, 64), slice(64, 128)
                lo_of(K2[h1, 0], kf[h0], K2[h0, 0])
                lo_of(K2[h0, 1], kf[h1], K2[h1, 1])
                lo_of(Q2l[h0, 0], qf[h0], Q2h[h0, 0])
                lo_of(Q2l[h1, 0], qf[h0], Q2h[h0, 0])
                lo_of(Q2l[h0, 1], qf[h1], Q2h[h1, 1])
                lo_of(Q2l[h1, 1], qf[h1], Q2h[h1, 1]).then_inc(sem["kq_lo"], 1)
                dve.wait_ge(sem["v_hi"], it + 1)
                vps = ps[:, 6:8, :].rearrange("p a (c h d) -> p (a c) h d", h=2, d=64)
                dve.tensor_tensor(V2[:, :, :, 64:128], vps, V2[:, :, :, 0:64].bitcast(F32), ALU.subtract).then_inc(sem["v_lo"], 1)

                dve.wait_ge(sem["hr_ready"], it + 1)
                link(dve.scalar_tensor_tensor(of[:], of[:], vec[:, bass.ds(it + V_HGRN, 1)], rf[:], ALU.mult, ALU.mult))
                dve.tensor_tensor(of[:], of[:], og[:], ALU.mult).then_inc(sem["y_f32"], 1)
                out_unit(4)
                dve.wait_ge(sem["y_hi_done"], it + 1)
                dve.tensor_tensor(ya_lo[:], of[:], ya_hi[:].bitcast(F32), ALU.subtract).then_inc(sem["y_lo_done"], 1)
                out_unit(5)

                n_diag = sum(SB_DIAGONAL)

                def neg_abs(s):
                    dve.wait_ge(sem["z_copied"], it * SB_N + s + 2)
                    if s >= 3:
                        dve.wait_ge(sem["cum1_done"], it * SB_N + s - 2)
                        dve.wait_ge(sem["cum2_done"], it * (SB_N - 2) + sum(j > 0 for _, j in SB_STEPS[:s - 2]))
                    z = zs[s % 3][:, :, sb_columns(s):]
                    dve.scalar_tensor_tensor(el[s % 3][:, :, sb_columns(s):], z, -1.0, z, ALU.mult, ALU.min)\
                       .then_inc(sem["nu_done"], 1)

                def softplus(s):
                    dve.wait_ge(sem["ln_done"], it * SB_N + s + 1)
                    e = el[s % 3][:, :, sb_columns(s):]
                    op = dve.scalar_tensor_tensor(e, zs[s % 3][:, :, sb_columns(s):], 0.0, e, ALU.max, ALU.add)
                    if SB_DIAGONAL[s]:
                        op.then_inc(sem["sp_pre"], 1)
                        dve.wait_ge(sem["sp_pre"], it * n_diag + sum(SB_DIAGONAL[:s]) + 1)
                        e = el[s % 3][:, :, sb_columns(s):sb_columns(s) + P]
                        op = dve.tensor_tensor(e, e, smask[:].unsqueeze(1).broadcast_to([P, 2, P]), ALU.mult)
                    op.then_inc(sem["sp_done"], 1)

                def softplus_lo(s):
                    dve.wait_ge(sem["sph_done"], it * SB_N + s + 1)
                    dve.tensor_tensor(spl[s % 3][:, :, sb_columns(s):], el[s % 3][:, :, sb_columns(s):],
                                      sph[s % 2][:, :, sb_columns(s):].bitcast(F32), ALU.subtract).then_inc(sem["spl_done"], 1)

                def log_a(s):
                    dve.wait_ge(sem["cum1_done"], it * SB_N + s + 1)
                    z = zs[s % 3][:, :, sb_columns(s):]
                    op = dve.tensor_tensor(z, z, ps[:, 4:6, sb_columns(s):HALF], ALU.add)
                    if SB_DIAGONAL[s]:
                        op.then_inc(sem["la_pre"], 1)
                        dve.wait_ge(sem["la_pre"], it * n_diag + sum(SB_DIAGONAL[:s]) + 1)
                        z = zs[s % 3][:, :, sb_columns(s):sb_columns(s) + P]
                        op = dve.tensor_tensor(z, z, negm[:].unsqueeze(1).broadcast_to([P, 2, P]), ALU.add)
                    op.then_inc(sem["la_done"], 1)

                def a_lo(s):
                    dve.wait_ge(sem["ah_done"], it * SB_N + s + 1)
                    if s:
                        dve.wait_ge(sem["av_done"], it * SB_N + s)
                    else:
                        dve.wait_ge(out_stored[0], it * 16 + 32)
                    dve.tensor_tensor(al[:, :, sb_columns(s):], zs[s % 3][:, :, sb_columns(s):], ah[:, :, sb_columns(s):].bitcast(F32),
                                      ALU.subtract).then_inc(sem["al_done"], 1)

                def leave_o(s):
                    dve.wait_ge(sem["av_done"], it * SB_N + s + 1)
                    dve.tensor_copy(ybf[0:64], ps[64:128, 6, :])
                    link(dve.tensor_copy(ybf[64:128], ps[64:128, 7, :]))
                    dve.tensor_tensor(ybf[0:64], ps[0:64, 6, :], ybf[0:64], ALU.add).then_inc(sem["yb_f32"], 1)
                    dve.tensor_tensor(ybf[64:128], ps[0:64, 7, :], ybf[64:128], ALU.add).then_inc(sem["yb_f32"], 1)

                def y_lo(c):
                    dve.wait_ge(sem["yb_hi"], it * 2 + c + 1)
                    cc = slice(c * HALF, (c + 1) * HALF)
                    dve.tensor_tensor(yb_lo[:, cc], ybf[:], yb_hi[:, cc].bitcast(F32), ALU.subtract).then_inc(sem["yb_lo"], 1)

                def leave_kv(i):
                    for w in range(kv_done(i), kv_done(i + 1)):
                        if w >= 4:
                            dve.wait_ge(kv_stored[w % 4], 16 * (w // 4))
                        leave(U + 6 + w, kvo[:, w % 4], ps[:, w % 2, 0:M], Rm)

                neg_abs(0)
                neg_abs(1)
                softplus(0)
                softplus_lo(0)
                for s in range(SB_N):
                    log_a(s)
                    if last:
                        leave_kv(2 * s)
                    elif s in (3, 6, 9):
                        leave(U + 5 + s // 3, (fq, qh, iv)[s // 3 - 1][:], wide(0))
                    if s == 4:
                        leave_o(3)
                    if s + 1 < SB_N:
                        softplus(s + 1)
                    if s + 2 < SB_N:
                        neg_abs(s + 2)
                    if s + 1 < SB_N:
                        softplus_lo(s + 1)
                    if last:
                        leave_kv(2 * s + 1)
                    a_lo(s)
                    if s == 5:
                        y_lo(0)
                if last:
                    leave_kv(2 * SB_N)
                else:
                    leave(U + 9, og[:], wide(0))
                leave_o(SB_N - 1)
                y_lo(1)
            with dve.Fori(0, HEADS - 1) as it:
                head_round(it, False)
            head_round(HEADS - 1, True)

            assert seq["n"] == LINKS, seq["n"]
            seq["base"], seq["n"] = seq0 + HEADS * LINKS, 0

            def one(t, n):
                return t[:, bass.ds(n, 1), :].rearrange("p o n -> p (o n)")

            for i in range(4):
                leave(U_TAIL + i, tail[:, i], wide(2 * (i % 2)))
            with dve.Fori(0, KT // 2) as p:
                for s in range(2):
                    n, u = p * 2 + s, p * 2 + (U_C + s)
                    dve.wait_ge(sem["unit_done"], u + 1)
                    dve.wait_ge(sem["gates_sig"], n * 2 + 2)
                    dve.tensor_tensor(t1[s][:], wide(4 * s), ga[s][:], ALU.mult).then_inc(sem["t1_done"], 1)
                    dve.tensor_tensor(t2[:], wide(4 * s + 2), gb[s][:], ALU.mult).then_inc(sem["pair_free"], 1)
                    dve.wait_ge(sem["t1_done"], n + 1)
                    dve.wait_ge(sem["pair_free"], u + 3)
                    dve.tensor_tensor(t1[s][:], t1[s][:], t2[:], ALU.add).then_inc(sem["m_done"], 1)
                    dve.wait_ge(sem["c_hi"], n + 1)
                    dve.tensor_tensor(one(A_lo, n), t1[s][:], one(A_hi, n).bitcast(F32),
                                      ALU.subtract).then_inc(sem["c_lo"], 1)

            def one(t, n):
                return t[:, bass.ds(n, 1), :].rearrange("p o n -> p (o n)")

            def residual(u0, k, g, olds, where):
                dve.wait_ge(sem["norm_pe"], k) if k else None
                dve.memset(SQ[:], 0.0).then_inc(sem["sqz"], 1)
                dve.wait_ge(sem["sqz"], k + 1)
                with dve.Fori(0, KT // 2) as p:
                    for s in range(2):
                        n = p * 2 + s
                        i = n + k * KT
                        dve.wait_ge(sem["unit_done"], n + (u0 + 1))
                        dve.wait_ge(olds[s], p * 16 + (16 + k * (KT // 2) * 16))
                        if k == 0:
                            dve.wait_ge(new_stored[s], p * 16 + 16)
                        dve.tensor_tensor(where(n, s), wide(2 * s), old[s][:], ALU.add).then_inc(sem["pair_free"], 1)
                        dve.wait_ge(sem["g_hi"], i + 1)
                        dve.scalar_tensor_tensor(one(B_lo, n), where(n, s), vec[:, bass.ds(n + g, 1)],
                                                 one(B_hi, n).bitcast(F32), ALU.mult, ALU.subtract).then_inc(sem["g_lo"], 1)
                        dve.wait_ge(sem["sq_done"], i + 1)
                        dve.tensor_tensor(SQ[:], SQ[:], sq[:], ALU.add).then_inc(sem["sq_acc"], 1)
                        dve.wait_ge(sem["sq_acc"], i + 2)

            def rms(k):
                dve.wait_ge(sem["norm_sqrt"], 2 + k)
                dve.reciprocal(R[:], sq[:]).then_inc(sem["r_ready"], 1)
                dve.wait_ge(sem["r_ready"], k)

            olds = old_in
            residual(U_D, 0, V_XATTN, olds, lambda n, s: new[s][:])
            rms(1)
            for t in new_stored:
                dve.wait_ge(t, (KT // 2 + 1) * 16)

            def queries(h, s):
                dve.wait_ge(sem["unit_done"], h * 2 + (U_E + 1 + s))
                dve.scalar_tensor_tensor(qx[:, s], wide(2 * s), 1.0 / 16, R[:], ALU.mult, ALU.mult)\
                   .then_inc(sem["pair_free"], 1)

            def weights_of(i):
                dve.wait_ge(sem["s_ready"], i + 1)
                s4 = ps[:, 4:6, :].rearrange("p a (t m) -> p (a t) m", m=M)
                dve.tensor_reduce(stat[:, 0, :], s4, AX_X, ALU.max).then_inc(sem["mx_done"], 1)
                dve.wait_ge(sem["mx_done"], i + 1)
                dve.tensor_scalar(stat[:, 1, :], stat[:, 0, :], -1.0, None, ALU.mult).then_inc(sem["nmx_done"], 1)
                dve.wait_ge(sem["p_exp"], i + 2)
                dve.reciprocal(stat[:, 3, :], stat[:, 2, :]).then_inc(sem["p_rec"], 1)
                dve.wait_ge(sem["p_rec"], i + 1)
                dve.tensor_tensor(px[:], px[:], stat[:, 3, :].unsqueeze(2).broadcast_to([P, 4, M]), ALU.mult)\
                   .then_inc(sem["p_done"], 1)

            def turned(i):
                dve.wait_ge(sem["pT_pe"], i + 1)
                dve.tensor_copy(pxT[:], ps[:, 6:8, :]).then_inc(sem["pT_done"], 1)

            def out_lo(h, hf):
                dve.wait_ge(sem["oE_hi"], h * 2 + (hf + 1))
                dst = (slice(None), bass.ds(h * 2, 2), slice(hf * HALF, (hf + 1) * HALF))
                dve.tensor_tensor(A_lo[dst], ps[:, 6:8, :], A_hi[dst].bitcast(F32), ALU.subtract).then_inc(sem["oE_lo"], 1)

            def attend(h, more):
                weights_of(h * 2)
                turned(h * 2)
                weights_of(h * 2 + 1)
                out_lo(h, 0)
                turned(h * 2 + 1)
                out_lo(h, 1)
                if more:
                    queries(h + 1, 0)
                    queries(h + 1, 1)

            queries(0, 0)
            queries(0, 1)
            with dve.Fori(0, HEADS - 1) as h:
                attend(h, True)
            attend(HEADS - 1, False)
            residual(U_F, 1, V_FFN, olds, lambda n, s: one(X, n))
            rms(2)
            u0 = U_G
            for gi, (f0, nf) in enumerate(GROUPS):
                with dve.Fori(0, nf) as f:
                    i = f + f0
                    dve.wait_ge(sem["unit_done"], f * 2 + (u0 + 1))
                    scaled(gt[:], wide(0), R[:]).then_inc(sem["pair_free"], 1)
                    dve.wait_ge(sem["unit_done"], f * 2 + (u0 + 2))
                    dve.wait_ge(sem["f_lo"], i + 1)
                    scaled(ut[:], wide(2), R[:]).then_inc(sem["pair_free"], 1)
                    dve.wait_ge(sem["f_silu"], i + 1)
                    dve.wait_ge(sem["pair_free"], f * 2 + (u0 + 4))
                    dve.tensor_tensor(ut[:], gt[:], ut[:], ALU.mult).then_inc(sem["f_prod"], 1)
                    dve.wait_ge(sem["f_hi"], i + 1)
                    dve.tensor_tensor(one(A_lo, f), ut[:], one(A_hi, f).bitcast(F32), ALU.subtract).then_inc(sem["f_lo"], 1)
                u1 = u0 + 2 * nf
                last = gi == len(GROUPS) - 1
                if last:
                    dve.memset(SQ[:], 0.0).then_inc(sem["sqz"], 1)
                    dve.wait_ge(sem["sqz"], 3)
                with dve.Fori(0, KT // 2) as p:
                    for s in range(2):
                        n = p * 2 + s
                        dve.wait_ge(sem["unit_done"], n + (u1 + 1))
                        dve.tensor_tensor(one(X, n), one(X, n), wide(2 * s), ALU.add).then_inc(sem["pair_free"], 1)
                        if last:
                            dve.wait_ge(sem["sq_done"], n + (2 * KT + 1))
                            dve.tensor_tensor(SQ[:], SQ[:], sq[:], ALU.add).then_inc(sem["sq_acc"], 1)
                            dve.wait_ge(sem["sq_acc"], n + (2 * KT + 2))
                u0 = u1 + KT
            rms(3)
            for n in range(KT):
                dve.scalar_tensor_tensor(X[:, n], X[:, n], vec[:, V_FINAL + n:V_FINAL + n + 1], R[:], ALU.mult, ALU.mult)\
                   .then_inc(sem["final_done"], 1)

        @block.scalar
        def _(act):
            def f(dst, src, func=ACT.Copy, **kw):
                return act.activation(dst, src, func, **kw)

            def waits_over():
                act.nop(nofuse=True)

            def one(t, n):
                return t[:, bass.ds(n, 1), :].rearrange("p o n -> p (o n)")

            def eps():
                return vec[:, V_EPS:V_EPS + 1]

            for t in out_stored + new_stored:
                act.sem_inc(t, 16)
            for n in ("y_stored", "yb_stored"):
                act.sem_inc(sem[n], 32)
            act.sem_inc(sem["z_copied"], 1)
            act.sem_inc(sem["p_exp"], 1)
            for c0, w, dst in ((C_MASK, (LEVELS + 1) * P, mask[:].rearrange("p a b -> p (a b)")), (C_RESET, T, reset[:]),
                               (C_SMASK, P, smask[:]), (C_NEGM, P, negm[:]), (C_ONES, P, ones[:]), (C_IDENT, P, ident[:]),
                               (C_NEGTRI, 2 * P, tri0[:].rearrange("p a b -> p (a b)"))):
                act.dma_start(dst, cst[:, c0:c0 + w]).then_inc(sem["cst_in"], 16)
            act.wait_ge(sem["vec_in"], 16)
            act.wait_ge(sem["lb_diff"], 1)
            f(lb[:, 1], lb[:, 1], ACT.Exp).then_inc(sem["lb_exp"], 1)
            f(lb[:, 2], lb[:, 2], ACT.Exp).then_inc(sem["lb_exp"], 1)

            def split_norm(src, g, hi, tmp, n, arrived):
                for k in range(KT):
                    act.wait_ge(*arrived(k))
                    f(hi[:, k], src[:, k], ACT.Copy, scale=vec[:, g + k:g + k + 1]).then_inc(sem[f"{n}_hi"], 1)
                    if k:
                        act.wait_ge(sem[f"{n}_sq"], k)
                    f(tmp[:], src[:, k], ACT.Square).then_inc(sem[f"{n}_sq_made"], 1)

            split_norm(x0, V_MIX, A_hi, sq0, "x", lambda k: (x_in[k // 2], 16))
            act.wait_ge(sem["norm0_pe"], 1)
            f(sq0[:], wide(4), ACT.Sqrt, scale=1.0 / D, bias=eps()).then_inc(sem["norm_sqrt"], 1)
            act.wait_ge(sem["cst_in"], 7 * 16)
            f(negtri[:], tri0[:, 0])
            f(negrest[:], tri0[:, 1]).then_inc(sem["consts_cast"], 1)
            split_norm(mem0, V_MEM, M0_hi, sqm, "m", lambda k: (sem["mem_in"], 16))
            act.wait_ge(sem["norm0_pe"], 2)
            f(sqm[:], ps[:, 6, 0:M], ACT.Sqrt, scale=1.0 / D, bias=eps()).then_inc(sem["norm_sqrt"], 1)
            act.wait_ge(sem["m_lo"], KT)
            act.dma_start(m_d[0], M0_hi[:].bitcast(F32)).then_inc(sem["m_stored"], 16)
            act.dma_start(m_d[1], M0_lo[:].bitcast(F32)).then_inc(sem["m_stored"], 16)
            act.wait_ge(sem["m_stored"], 32)

            def head_round(it, last):
                U = it * PER_IT + PROLOGUE

                def left(i):
                    act.wait_ge(sem["pair_free"], U + (i + 3))

                left(-1)
                f(fq[:], fq[:], ACT.Sigmoid).then_inc(sem["hgrn_sig"], 1)
                f(El[1][:], qh[:], ACT.Sigmoid).then_inc(sem["hgrn_sig"], 1)
                f(QK[0][:], og[:], ACT.Sigmoid).then_inc(sem["hgrn_sig"], 1)
                act.preload_act_table_set("natural_log_exp_and_others")
                act.wait_ge(sem["hgrn_f"], it + 1)
                f(QK[1][:], bb[:], ACT.Ln).then_inc(sem["hgrn_lf"], 1)
                act.wait_ge(sem["iT_done"], it + 1)
                f(vtok[:].rearrange("p c v -> p (c v)"), wide(4)).then_inc(sem["vtok_copied"], 1)
                for lev in range(LEVELS):
                    m = CH >> (lev + 1)
                    act.wait_ge(sem["d_ready"], it * (LEVELS + 1) + lev + 1)
                    if lev >= 2:
                        act.wait_ge(sem["qk_ready"], it * LEVELS + lev - 1)
                    d, e = (x[:].rearrange("p (n h m) -> p n h m", h=2, m=m) for x in (Dl[lev % 2], El[lev % 2]))
                    f(e[:, :, 0], d[:, :, 0], ACT.Exp, scale=-1.0)
                    f(e[:, :, 1], d[:, :, 1], ACT.Exp).then_inc(sem["e_ready"], 1)
                act.wait_ge(sem["qk_ready"], it * LEVELS + LEVELS - 1)
                f(El[1][:], bb[:], ACT.Exp).then_inc(sem["e_ready"], 1)
                act.wait_ge(sem["d_ready"], it * (LEVELS + 1) + LEVELS + 1)
                act.wait_ge(sem["qk_ready"], it * LEVELS + LEVELS)
                f(El[0][:], Dl[0][:], ACT.Exp).then_inc(sem["e_ready"], 1)
                act.wait_ge(sem["keT_done"], it + 1)
                f(Ketok[:].rearrange("p c v -> p (c v)"), wide(6)).then_inc(sem["keT_copied"], 1)
                act.wait_ge(sem["o_done"], it + 1)
                f(of[:], wide(6))
                f(QK[1][:], wide(6), ACT.Square).then_inc(sem["osq_ready"], 1)

                def store(w):
                    left(w)
                    s = w % 2
                    act.dma_start(row(gate_d, it * 3 + (w - 3)), outr[:, s]).then_inc(out_stored[s], 16)

                h0, h1 = slice(0, 64), slice(64, 128)
                for dst, src in ((K2[h0, 0], kf[h0]), (K2[h1, 1], kf[h1]), (Q2h[h0, 0], qf[h0]), (Q2h[h1, 0], qf[h0]),
                                 (Q2h[h1, 1], qf[h1]), (Q2h[h0, 1], qf[h1])):
                    f(dst, src).then_inc(sem["kq_hi"], 1)
                act.wait_ge(sem["vT_done"], it + 1)
                vps = ps[:, 6:8, :].rearrange("p a (c h d) -> p (a c) h d", h=2, d=64)
                f(V2[:, :, :, 0:64], vps).then_inc(sem["v_hi"], 1)
                act.wait_ge(sem["hms_done"], it + 1)
                f(rf[:], wide(4), ACT.Ln, scale=1.0 / P, bias=eps()).then_inc(sem["hln"], 1)
                act.wait_ge(sem["hln"], it + 1)
                f(rf[:], rf[:], ACT.Exp, scale=-0.5).then_inc(sem["hr_ready"], 1)
                store(3)
                act.wait_ge(sem["y_f32"], it + 1)
                f(ya_hi[:], of[:]).then_inc(sem["y_hi_done"], 1)
                if last:
                    act.wait_ge(sem["s_done"], (it + 1) * (LEVELS + 1))
                    for i, m in enumerate((M_hi, M_lo)):
                        act.dma_start(m[:].bitcast(F32), m_d[i]).then_inc(sem["m_loaded"], 16)
                store(4)
                act.wait_ge(sem["y_lo_done"], it + 1)
                act.dma_start(row(y_d[0], it), ya_hi[:].bitcast(F32)).then_inc(sem["y_stored"], 16)
                act.dma_start(row(y_d[1], it), ya_lo[:].bitcast(F32)).then_inc(sem["y_stored"], 16)
                store(5)

                def copy_z(s):
                    if s >= 3:
                        act.wait_ge(sem["al_done"], it * SB_N + s - 2)
                    act.wait_ge(sem["z_done"], it * SB_N + s + 1)
                    f(zs[s % 3][:, :, sb_columns(s):], ps[:, 2:4, sb_columns(s):HALF]).then_inc(sem["z_copied"], 1)

                def exp_nu(s):
                    act.wait_ge(sem["nu_done"], it * SB_N + s + 1)
                    e = el[s % 3][:, :, sb_columns(s):]
                    f(e, e, ACT.Exp).then_inc(sem["ex_done"], 1)

                def ln_one(s):
                    act.wait_ge(sem["ex_done"], it * SB_N + s + 1)
                    e = el[s % 3][:, :, sb_columns(s):]
                    f(e, e, ACT.Ln, bias=1.0).then_inc(sem["ln_done"], 1)

                def softplus_hi(s):
                    act.wait_ge(sem["sp_done"], it * SB_N + s + 1)
                    if s >= 2:
                        act.wait_ge(sem["cum1_done"], it * SB_N + s - 1)
                        act.wait_ge(sem["cum2_done"], it * (SB_N - 2) + sum(j > 0 for _, j in SB_STEPS[:s - 1]))
                    if s == 1:
                        act.wait_ge(sem["y_stored"], it * 32 + 64)
                    f(sph[s % 2][:, :, sb_columns(s):], el[s % 3][:, :, sb_columns(s):]).then_inc(sem["sph_done"], 1)

                def exp_a(s):
                    act.wait_ge(sem["la_done"], it * SB_N + s + 1)
                    z = zs[s % 3][:, :, sb_columns(s):]
                    f(z, z, ACT.Exp).then_inc(sem["a_done"], 1)

                def a_hi(s):
                    act.wait_ge(sem["a_done"], it * SB_N + s + 1)
                    if s:
                        act.wait_ge(sem["av_done"], it * SB_N + s)
                    f(ah[:, :, sb_columns(s):], zs[s % 3][:, :, sb_columns(s):]).then_inc(sem["ah_done"], 1)

                def y_hi(c):
                    act.wait_ge(sem["yb_f32"], it * 4 + 2 * c + 6)
                    f(yb_hi[:, c * HALF:(c + 1) * HALF], ybf[:]).then_inc(sem["yb_hi"], 1)

                def store_kv(i0, i1):
                    for w in range(kv_done(i0), kv_done(i1)):
                        left(6 + w)
                        act.dma_start(kv_d[w], kvo[:, w % 4]).then_inc(kv_stored[w % 4], 16)

                copy_z(0)
                exp_nu(0)
                copy_z(1)
                ln_one(0)
                exp_nu(1)
                softplus_hi(0)
                ln_one(1)
                for s in range(SB_N):
                    if s + 2 < SB_N:
                        copy_z(s + 2)
                    exp_a(s)
                    if s + 1 < SB_N:
                        softplus_hi(s + 1)
                    if s + 2 < SB_N:
                        exp_nu(s + 2)
                    a_hi(s)
                    if s + 2 < SB_N:
                        ln_one(s + 2)
                    if last:
                        store_kv(max(0, 2 * s), 2 * s + 1)
                        store_kv(2 * s + 1, 2 * s + 2)
                    if s == 4:
                        y_hi(0)
                if last:
                    store_kv(2 * SB_N, 2 * SB_N + 1)
                y_hi(1)
                act.wait_ge(sem["yb_lo"], it * 2 + 2)
                act.dma_start(row(y_d[0], it + HEADS), yb_hi[:].bitcast(F32)).then_inc(sem["yb_stored"], 16)
                act.dma_start(row(y_d[1], it + HEADS), yb_lo[:].bitcast(F32)).then_inc(sem["yb_stored"], 16)

            with act.Fori(0, HEADS - 1) as it:
                head_round(it, False)
            head_round(HEADS - 1, True)

            act.wait_ge(sem["y_stored"], (HEADS + 1) * 32)
            act.wait_ge(sem["yb_stored"], (HEADS + 1) * 32)
            act.wait_ge(out_stored[0], 16 * (HEADS + 1))
            act.wait_ge(out_stored[1], 16 * (2 * HEADS + 1))
            for t in kv_stored:
                act.wait_ge(t, 2 * KT // 4 * 16)
            act.wait_ge(sem["av_done"], HEADS * SB_N)
            act.dma_start(B_hi[:].bitcast(F32), y_d[0].rearrange("k p t -> p k t")).then_inc(sem["y_loaded"], 16)
            act.dma_start(B_lo[:].bitcast(F32), y_d[1].rearrange("k p t -> p k t")).then_inc(sem["y_loaded"], 16)

            def load_gates(n, s):
                act.dma_start(ga[s][:], row(gate_d, n)).then_inc(ga_in[s], 16)
                act.dma_start(gb[s][:], row(gate_d, n + KT)).then_inc(gb_in[s], 16)

            for s in range(2):
                load_gates(s, s)
            for i in range(4):
                act.wait_ge(sem["pair_free"], U_TAIL + i + 3)
                act.dma_start(gate_d[12 + i], tail[:, i]).then_inc(sem["tail_stored"], 16)
            act.wait_ge(sem["tail_stored"], 64)
            def gate_tiles(p, more):
                for s in range(2):
                    n = p * 2 + s
                    act.wait_ge(ga_in[s], p * 16 + 16)
                    f(ga[s][:], ga[s][:], ACT.Sigmoid).then_inc(sem["gates_sig"], 1)
                    act.wait_ge(gb_in[s], p * 16 + 16)
                    f(gb[s][:], gb[s][:], ACT.Sigmoid).then_inc(sem["gates_sig"], 1)
                    act.wait_ge(sem["m_done"], n + 1)
                    waits_over()
                    f(one(A_hi, n), t1[s][:]).then_inc(sem["c_hi"], 1)
                    if more:
                        load_gates(n + 2, s)

            with act.Fori(0, KT // 2 - 1) as p:
                gate_tiles(p, True)
            gate_tiles(KT // 2 - 1, False)

            def residual(u0, k, g, src, where, store_new):
                act.wait_ge(sem["unit_done"], u0)
                for s in range(2):
                    act.dma_start(old[s][:], src(s)).then_inc(old_in[s], 16)

                def tiles(p, more):
                    for s in range(2):
                        n = p * 2 + s
                        act.wait_ge(sem["pair_free"], n + (u0 + 3))
                        if more:
                            act.dma_start(old[s][:], src(n + 2)).then_inc(old_in[s], 16)
                        if store_new:
                            act.dma_start(row(x1_d, n), where(n, s)).then_inc(new_stored[s], 16)
                        waits_over()
                        f(one(B_hi, n), where(n, s), ACT.Copy, scale=vec[:, bass.ds(n + g, 1)]).then_inc(sem["g_hi"], 1)
                        act.wait_ge(sem["sq_acc"], n + (k * KT + 1))
                        waits_over()
                        f(sq[:], where(n, s), ACT.Square).then_inc(sem["sq_done"], 1)

                with act.Fori(0, KT // 2 - 1) as p:
                    tiles(p, True)
                tiles(KT // 2 - 1, False)

            def rms(k):
                act.wait_ge(sem["norm_pe"], k)
                f(sq[:], wide(4), ACT.Sqrt, scale=1.0 / D, bias=eps()).then_inc(sem["norm_sqrt"], 1)

            residual(U_D, 0, V_XATTN, lambda n: one(xT, n), lambda n, s: new[s][:], True)
            rms(1)

            for t in new_stored:
                act.wait_ge(t, (KT // 2 + 1) * 16)
            act.dma_start(kx[:], kv_d[0:KT].rearrange("k p m -> p k m")).then_inc(sem["kx_in"], 16)

            def load_v(h):
                act.dma_start(vx[:], kv_d[bass.ds(h * 2 + KT, 2)].rearrange("k p m -> p k m")).then_inc(sem["vx_in"], 16)

            load_v(0)

            def attend(h, more):
                act.wait_ge(sem["vtokE_pe"], h + 1)
                if more:
                    load_v(h + 1)
                f(vxt[:].rearrange("p a m -> p (a m)"), ps[:, 6, :]).then_inc(sem["vtokE_done"], 1)
                for hf in range(2):
                    i = h * 2 + hf
                    act.wait_ge(sem["nmx_done"], i + 1)
                    if hf:
                        act.wait_ge(sem["pT_pe"], i)
                    for tt in range(4):
                        ins = f(px[:, tt], ps[:, 4 + tt // 2, (tt % 2) * M:(tt % 2 + 1) * M], ACT.Exp,
                                bias=stat[:, 1, tt:tt + 1], accum_out=stat[:, 2, tt:tt + 1])
                    ins.then_inc(sem["p_exp"], 1)
                    act.wait_ge(sem["oE_pe"], i + 1)
                    waits_over()
                    f(A_hi[:, bass.ds(h * 2, 2), hf * HALF:(hf + 1) * HALF], ps[:, 6:8, :]).then_inc(sem["oE_hi"], 1)

            with act.Fori(0, HEADS - 1) as h:
                attend(h, True)
            attend(HEADS - 1, False)
            residual(U_F, 1, V_FFN, lambda n: row(x1_d, n), lambda n, s: one(X, n), False)
            rms(2)
            u0 = U_G
            for gi, (f0, nf) in enumerate(GROUPS):
                with act.Fori(0, nf) as ff:
                    act.wait_ge(sem["pair_free"], ff * 2 + (u0 + 3))
                    f(gt[:], gt[:], ACT.Silu).then_inc(sem["f_silu"], 1)
                    act.wait_ge(sem["f_prod"], ff + (f0 + 1))
                    waits_over()
                    f(one(A_hi, ff), ut[:]).then_inc(sem["f_hi"], 1)
                u1 = u0 + 2 * nf
                if gi == len(GROUPS) - 1:
                    with act.Fori(0, KT) as n:
                        act.wait_ge(sem["pair_free"], n + (u1 + 3))
                        act.wait_ge(sem["sq_acc"], n + (2 * KT + 1))
                        waits_over()
                        f(sq[:], one(X, n), ACT.Square).then_inc(sem["sq_done"], 1)
                u0 = u1 + KT
            rms(3)
            for n in range(KT):
                act.wait_ge(sem["final_done"], n + 1)
                act.dma_start(out[n], X[:, n]).then_inc(sem["stored"], 16)
            act.wait_ge(sem["stored"], KT * 16)


def _tiles(w, n):
    c = w[:, n * P:(n + 1) * P].reshape(-1, P, P).transpose(1, 0, 2)
    u = np.zeros((P, KT, P), np.float32)
    u[:, :c.shape[1]] = c
    return u.reshape(P, D)


def _stream(w_in, w_gate, w_proj_a, w_proj_b, w_out, w_xq, w_xkv, w_xo, w_ffn_in, w_ffn_out):
    units = []
    col = lambda part, h: part * HEADS + h
    def fqio(h):
        return [_tiles(w_in, col(part, h)) for part in (1, 0, 2, 3)]

    units += fqio(0)
    for h in range(HEADS):
        units += [_tiles(w_in, col(part, h)) for part in (4, 5, 6)]
        units += [_tiles(w_gate, 3 * h + g) for g in range(3)]
        units += fqio(h + 1) if h + 1 < HEADS else [_tiles(w_xkv, n) for n in range(2 * KT)]
    units += [_tiles(w_gate, 12 + g) for g in range(4)]
    for w in (np.concatenate([w_proj_a, w_proj_b], 0), w_out, w_xq, w_xo):
        units += [_tiles(w, n) for n in range(KT)]
    for f0, nf in GROUPS:
        for f in range(f0, f0 + nf):
            units += [_tiles(w_ffn_in, f), _tiles(w_ffn_in, FT + f)]
        units += [_tiles(w_ffn_out[f0 * P:(f0 + nf) * P], n) for n in range(KT)]
    return np.stack(units)


def kernel(x, mem, g_mix, w_in, lb_table, g_hgrn, w_gate, w_proj_a, w_proj_b, w_out,
           g_xattn, g_mem, w_xq, w_xkv, w_xo, g_ffn, w_ffn_in, w_ffn_out, g_final):
    import concourse.bacc as bacc
    from concourse.bass_utils import run_bass_kernel_spmd

    def a(v):
        return np.ascontiguousarray(v)

    def feature_major(v):
        return np.ascontiguousarray(a(v)[0].T.reshape(KT, P, -1).transpose(1, 0, 2))

    def columns(v):
        return a(v).reshape(-1, P).T

    vecs = np.concatenate([columns(v) for v in (g_mix, g_xattn, g_mem, g_ffn, g_final, g_hgrn, a(lb_table)[0], a(lb_table)[1])]
                          + [np.full((P, V_ALL - V_EPS), EPS, np.float32)], 1)
    arrays = {
        "x_t": feature_major(x), "mem_t": feature_major(mem), "vectors": np.ascontiguousarray(vecs), "constants": constants(),
        "weights": _stream(*(a(w)[0] for w in (w_in, w_gate, w_proj_a, w_proj_b, w_out, w_xq, w_xkv, w_xo, w_ffn_in, w_ffn_out))),
    }
    nc = bacc.Bacc("TRN2", target_bir_lowering=False, num_devices=1)
    args = [nc.dram_tensor(n, v.shape, F32, kind="ExternalInput").ap() for n, v in arrays.items()]
    out = nc.dram_tensor("out_t", (KT, P, T), F32, kind="ExternalOutput").ap()
    build(nc, *args, out)
    r = run_bass_kernel_spmd(nc, [arrays], core_ids=[0])
    return np.ascontiguousarray(r.results[0]["out_t"].reshape(D, T).T)[None]
```
